# Optimizing a Trainium2 kernel written in Bass

```python
import math
import jax
import jax.numpy as jnp
from jax import lax
import numpy as np

D_MODEL = 1024
BATCH = 1
SEQ = 256
DEPTH = 2

EPS = 1e-6
ROPE_THETA = 10000.0
MIX_WIDTH = 1024
RET_HEADS = 4
RET_HEAD_DIM = 128
RET_WIDTH = RET_HEADS * RET_HEAD_DIM
RET_CHUNK = 128
HGRN_HEADS = 4
HGRN_DK = 128
HGRN_DV = 128
HGRN_WIDTH = HGRN_HEADS * HGRN_DK
HGRN_CHUNK = 64
AB_IN = 4 * RET_WIDTH + 4 * HGRN_WIDTH
SB_HEADS = 4
SB_HEAD_DIM = 128
SB_WIDTH = SB_HEADS * SB_HEAD_DIM
DIFF_HEADS = 4
DIFF_QK_DIM = 64
DIFF_V_DIM = 128
DIFF_WIDTH = DIFF_HEADS * DIFF_V_DIM
CD_IN = 3 * SB_WIDTH + 3 * DIFF_WIDTH
Q_BLOCK = 128
N_GROUPS = 4
EXPERTS_PER_GROUP = 8
N_EXPERTS = N_GROUPS * EXPERTS_PER_GROUP
TOP_K = 2
EXPERT_FF = 512
ROW_BLOCK = 256

kernel_name = "hybrid_ret_hgrn2_stickbreak_diffattn_hiermoe"

F32 = jnp.float32

def rms_norm(x, gain):
    xf = x.astype(F32)
    y = xf * lax.rsqrt(jnp.mean(xf * xf, axis=-1, keepdims=True) + EPS)
    return (y * gain.astype(F32)).astype(x.dtype)

def rope_tables(positions, dim):
    inv = 1.0 / (ROPE_THETA ** (jnp.arange(0, dim, 2, dtype=F32) / dim))
    ang = positions.astype(F32)[..., None] * inv
    return jnp.cos(ang), jnp.sin(ang)

def apply_rope(x, cos, sin):
    xf = x.astype(F32)
    half = xf.shape[-1] // 2
    x1, x2 = xf[..., :half], xf[..., half:]
    return jnp.concatenate([x1 * cos - x2 * sin, x2 * cos + x1 * sin], axis=-1)

def _chunks(t, n, c):
    b, s, h, d = t.shape
    return t.astype(F32).reshape(b, n, c, h, d).transpose(1, 0, 3, 2, 4)

def retention_chunkwise(q, k, v):
    B, S, H, d = q.shape
    C = RET_CHUNK
    N = S // C
    log_gamma = jnp.log(1.0 - 2.0 ** (-5.0 - jnp.arange(H, dtype=F32)))
    qc = _chunks(q, N, C) * (d ** -0.5)
    kc = _chunks(k, N, C)
    vc = _chunks(v, N, C)
    idx = jnp.arange(C, dtype=F32)
    rel = idx[:, None] - idx[None, :]
    decay = jnp.where(rel >= 0, jnp.exp(log_gamma[:, None, None] * jnp.maximum(rel, 0.0)), 0.0)
    q_decay = jnp.exp(log_gamma[:, None] * (idx + 1.0))[:, :, None]
    k_decay = jnp.exp(log_gamma[:, None] * (C - 1.0 - idx))[:, :, None]
    chunk_decay = jnp.exp(log_gamma * C)[:, None, None]

    def step(state, inp):
        qi, ki, vi = inp
        scores = jnp.einsum('bhtd,bhsd->bhts', qi, ki) * decay
        inner = jnp.einsum('bhts,bhse->bhte', scores, vi)
        cross = jnp.einsum('bhtd,bhde->bhte', qi, state) * q_decay
        state = state * chunk_decay + jnp.einsum('bhsd,bhse->bhde', ki * k_decay, vi)
        return state, inner + cross

    state0 = jnp.zeros((B, H, d, v.shape[-1]), F32)
    _, out = lax.scan(step, state0, (qc, kc, vc))
    return out.transpose(1, 0, 3, 2, 4).reshape(B, S, H, -1)

def hgrn2_chunkwise(q, k, v, log_f):
    B, S, H, dk = q.shape
    C = HGRN_CHUNK
    N = S // C
    qc = _chunks(q, N, C) * (dk ** -0.5)
    kc = _chunks(k, N, C)
    vc = _chunks(v, N, C)
    gc = _chunks(log_f, N, C)
    causal = jnp.tril(jnp.ones((C, C), dtype=bool))[:, :, None]

    def step(state, inp):
        qi, ki, vi, gi = inp
        b = jnp.cumsum(gi, axis=2)
        diff = b[:, :, :, None, :] - b[:, :, None, :, :]
        w = jnp.exp(jnp.where(causal, diff, -jnp.inf))
        scores = jnp.einsum('bhtd,bhtsd->bhts', qi, w * ki[:, :, None, :, :])
        inner = jnp.einsum('bhts,bhse->bhte', scores, vi)
        cross = jnp.einsum('bhtd,bhde->bhte', qi * jnp.exp(b), state)
        b_last = b[:, :, -1:, :]
        state = state * jnp.swapaxes(jnp.exp(b_last), 2, 3) + jnp.einsum(
            'bhsd,bhse->bhde', ki * jnp.exp(b_last - b), vi)
        return state, inner + cross

    state0 = jnp.zeros((B, H, dk, v.shape[-1]), F32)
    _, out = lax.scan(step, state0, (qc, kc, vc, gc))
    return out.transpose(1, 0, 3, 2, 4).reshape(B, S, H, -1)

def stick_breaking_attention(q, k, v):
    S = q.shape[2]
    scale = q.shape[-1] ** -0.5
    outs = []
    for i0 in range(0, S, Q_BLOCK):
        i1 = i0 + Q_BLOCK
        z = jnp.einsum('bhqd,bhkd->bhqk', q[:, :, i0:i1], k[:, :, :i1]).astype(F32) * scale
        mask = jnp.arange(i1)[None, :] < jnp.arange(i0, i1)[:, None]
        log_beta = jax.nn.log_sigmoid(z)
        log_1mb = jnp.where(mask, jax.nn.log_sigmoid(-z), 0.0)
        after = lax.cumsum(log_1mb, axis=3, reverse=True) - log_1mb
        a = jnp.where(mask, jnp.exp(log_beta + after), 0.0)
        outs.append(jnp.einsum('bhqk,bhkd->bhqd', a, v[:, :, :i1].astype(F32)))
    return jnp.concatenate(outs, axis=2)

def differential_attention(q, k, v, lam):
    S = q.shape[3]
    scale = q.shape[-1] ** -0.5
    outs = []
    for i0 in range(0, S, Q_BLOCK):
        i1 = i0 + Q_BLOCK
        s = jnp.einsum('bhcqd,bhckd->bhcqk', q[:, :, :, i0:i1], k[:, :, :, :i1]).astype(F32) * scale
        mask = jnp.arange(i1)[None, :] <= jnp.arange(i0, i1)[:, None]
        p = jax.nn.softmax(jnp.where(mask, s, -jnp.inf), axis=-1)
        a = p[:, :, 0] - lam * p[:, :, 1]
        outs.append(jnp.einsum('bhqk,bhkd->bhqd', a, v[:, :, :i1].astype(F32)))
    return jnp.concatenate(outs, axis=2)

def retention_hgrn2_mixer(h, w_in, w_out, ret_gain, lb, hgrn_gain, cos, sin):
    B, S, _ = h.shape
    proj = h @ w_in
    rq, rk, rv, rg, hq, hf, hi, hg = jnp.split(proj, 8, axis=-1)
    rshape = (B, S, RET_HEADS, RET_HEAD_DIM)
    rq = apply_rope(rq.reshape(rshape), cos[:, :, None], sin[:, :, None])
    rk = apply_rope(rk.reshape(rshape), cos[:, :, None], sin[:, :, None])
    ret = retention_chunkwise(rq, rk, rv.reshape(rshape))
    ret = rms_norm(ret, ret_gain).reshape(B, S, RET_WIDTH) * jax.nn.silu(rg.astype(F32))
    hshape = (B, S, HGRN_HEADS, HGRN_DK)
    lb = lb.reshape(HGRN_HEADS, HGRN_DK)
    f_raw = hf.astype(F32).reshape(hshape)
    log_f = jnp.log(lb + (1.0 - lb) * jax.nn.sigmoid(f_raw))
    hk = (1.0 - lb) * jax.nn.sigmoid(-f_raw)
    hq = jax.nn.silu(hq.astype(F32)).reshape(hshape)
    hv = hi.astype(F32).reshape(B, S, HGRN_HEADS, HGRN_DV)
    o = hgrn2_chunkwise(hq, hk, hv, log_f)
    o = rms_norm(o, hgrn_gain).reshape(B, S, HGRN_HEADS * HGRN_DV) * jax.nn.silu(hg.astype(F32))
    mixed = jnp.concatenate([ret, o], axis=-1).astype(h.dtype)
    return mixed @ w_out

def stickbreak_diff_mixer(h, w_in, w_out, q_gain, k_gain, lq1, lk1, lq2, lk2, subln, cos, sin, layer_idx):
    B, S, _ = h.shape
    proj = h @ w_in
    sq, sk, sv, dq, dk, dv = jnp.split(proj, 6, axis=-1)
    sshape = (B, S, SB_HEADS, SB_HEAD_DIM)
    sq, sk, sv = [t.reshape(sshape).transpose(0, 2, 1, 3) for t in (sq, sk, sv)]
    sb = stick_breaking_attention(sq, sk, sv)
    sb = sb.transpose(0, 2, 1, 3).reshape(B, S, SB_WIDTH)
    dshape = (B, S, DIFF_HEADS, 2, DIFF_QK_DIM)
    dq = apply_rope(rms_norm(dq.reshape(dshape), q_gain), cos[:, :, None, None], sin[:, :, None, None])
    dk = apply_rope(rms_norm(dk.reshape(dshape), k_gain), cos[:, :, None, None], sin[:, :, None, None])
    dq = dq.transpose(0, 2, 3, 1, 4)
    dk = dk.transpose(0, 2, 3, 1, 4)
    dv = dv.reshape(B, S, DIFF_HEADS, DIFF_V_DIM).transpose(0, 2, 1, 3)
    lam_init = 0.8 - 0.6 * math.exp(-0.3 * layer_idx)
    lam = (jnp.exp(jnp.sum(lq1.astype(F32) * lk1.astype(F32)))
           - jnp.exp(jnp.sum(lq2.astype(F32) * lk2.astype(F32))) + lam_init)
    da = differential_attention(dq, dk, dv, lam)
    da = rms_norm(da, subln) * (1.0 - lam_init)
    da = da.transpose(0, 2, 1, 3).reshape(B, S, DIFF_WIDTH)
    mixed = jnp.concatenate([sb, da], axis=-1).astype(h.dtype)
    return mixed @ w_out

def hierarchical_moe(h, wg_r, bg_r, we_r, be_r, w_gate, w_up, w_down):
    B, S, D = h.shape
    T = B * S
    M = T * TOP_K
    hf = h.reshape(T, D)
    g_logits = (hf @ wg_r).astype(F32) + bg_r.astype(F32)
    p_group = jax.nn.softmax(g_logits, axis=-1)
    g_sel = jnp.argmax(g_logits, axis=-1)
    p_g = jnp.take_along_axis(p_group, g_sel[:, None], axis=1)
    e_logits = ((hf @ we_r).astype(F32) + be_r.astype(F32)).reshape(T, N_GROUPS, EXPERTS_PER_GROUP)
    e_in = jnp.take_along_axis(e_logits, g_sel[:, None, None], axis=1)[:, 0]
    top_v, top_i = lax.top_k(e_in, TOP_K)
    gate = p_g * jax.nn.softmax(top_v, axis=-1)
    expert = g_sel[:, None] * EXPERTS_PER_GROUP + top_i
    flat_e = expert.reshape(M)
    flat_w = gate.reshape(M)
    order = jnp.argsort(flat_e)
    sorted_e = flat_e[order]
    tok = order // TOP_K
    counts = jnp.bincount(flat_e, length=N_EXPERTS)
    padded = (counts + ROW_BLOCK - 1) // ROW_BLOCK * ROW_BLOCK
    start = jnp.cumsum(counts) - counts
    pstart = jnp.cumsum(padded) - padded
    pend = pstart + padded
    dest = pstart[sorted_e] + (jnp.arange(M) - start[sorted_e])
    n_blocks = -(-M // ROW_BLOCK) + N_EXPERTS
    P = n_blocks * ROW_BLOCK
    xs = jnp.zeros((P, D), hf.dtype).at[dest].set(hf[tok])
    block_start = jnp.arange(n_blocks) * ROW_BLOCK
    block_e = jnp.minimum(jnp.searchsorted(pend, block_start, side='right'), N_EXPERTS - 1)

    def expert_block(args):
        xb, e = args
        a = jax.nn.silu(xb @ w_gate[e]) * (xb @ w_up[e])
        return a @ w_down[e]

    y = lax.map(expert_block, (xs.reshape(n_blocks, ROW_BLOCK, D), block_e)).reshape(P, D)
    y_rows = y[dest] * flat_w[order][:, None].astype(y.dtype)
    out = jax.ops.segment_sum(y_rows, tok, num_segments=T)
    return out.reshape(B, S, D)

def setup_inputs(seed: int = 0) -> dict:
    key = jax.random.key(seed)
    ks = jax.random.split(key, 32)
    n_ab = (DEPTH + 1) // 2
    n_cd = DEPTH // 2

    def nrm(k, shape, scale):
        return jax.random.normal(k, shape, F32) * scale

    def gain(k, shape):
        return 1.0 + 0.02 * jax.random.normal(k, shape, F32)

    x = nrm(ks[0], (BATCH, SEQ, D_MODEL), 1.0)
    offset = jax.random.randint(ks[1], (BATCH, 1), 0, 1024)
    positions = (offset + jnp.arange(SEQ)[None, :]).astype(jnp.int32)
    return {
        "x": x,
        "positions": positions,
        "norm_mix": gain(ks[2], (DEPTH, D_MODEL)),
        "norm_ffn": gain(ks[3], (DEPTH, D_MODEL)),
        "w_in_ab": nrm(ks[4], (n_ab, D_MODEL, AB_IN), D_MODEL ** -0.5),
        "w_out_ab": nrm(ks[5], (n_ab, MIX_WIDTH, D_MODEL), MIX_WIDTH ** -0.5),
        "ret_gnorm": gain(ks[6], (n_ab, RET_HEADS, RET_HEAD_DIM)),
        "hgrn_lb_logits": nrm(ks[7], (DEPTH + 1, HGRN_WIDTH), 0.1),
        "hgrn_onorm": gain(ks[8], (n_ab, HGRN_HEADS, HGRN_DV)),
        "w_in_cd": nrm(ks[9], (n_cd, D_MODEL, CD_IN), D_MODEL ** -0.5),
        "w_out_cd": nrm(ks[10], (n_cd, MIX_WIDTH, D_MODEL), MIX_WIDTH ** -0.5),
        "diff_qnorm": gain(ks[11], (n_cd, DIFF_QK_DIM)),
        "diff_knorm": gain(ks[12], (n_cd, DIFF_QK_DIM)),
        "diff_lam_q1": nrm(ks[13], (n_cd, DIFF_QK_DIM), 0.1),
        "diff_lam_k1": nrm(ks[14], (n_cd, DIFF_QK_DIM), 0.1),
        "diff_lam_q2": nrm(ks[15], (n_cd, DIFF_QK_DIM), 0.1),
        "diff_lam_k2": nrm(ks[16], (n_cd, DIFF_QK_DIM), 0.1),
        "diff_subln": gain(ks[17], (n_cd, DIFF_V_DIM)),
        "router_group_w": nrm(ks[18], (DEPTH, D_MODEL, N_GROUPS), D_MODEL ** -0.5),
        "router_group_b": nrm(ks[19], (DEPTH, N_GROUPS), 0.01),
        "router_expert_w": nrm(ks[20], (DEPTH, D_MODEL, N_EXPERTS), D_MODEL ** -0.5),
        "router_expert_b": nrm(ks[21], (DEPTH, N_EXPERTS), 0.01),
        "w_gate": nrm(ks[22], (DEPTH, N_EXPERTS, D_MODEL, EXPERT_FF), D_MODEL ** -0.5),
        "w_up": nrm(ks[23], (DEPTH, N_EXPERTS, D_MODEL, EXPERT_FF), D_MODEL ** -0.5),
        "w_down": nrm(ks[24], (DEPTH, N_EXPERTS, EXPERT_FF, D_MODEL), EXPERT_FF ** -0.5),
    }

def reference(x, positions, norm_mix, norm_ffn, w_in_ab, w_out_ab, ret_gnorm, hgrn_lb_logits,
              hgrn_onorm, w_in_cd, w_out_cd, diff_qnorm, diff_knorm, diff_lam_q1, diff_lam_k1,
              diff_lam_q2, diff_lam_k2, diff_subln, router_group_w, router_group_b,
              router_expert_w, router_expert_b, w_gate, w_up, w_down):
    cos_r, sin_r = rope_tables(positions, RET_HEAD_DIM)
    cos_d, sin_d = rope_tables(positions, DIFF_QK_DIM)
    lb_table = jnp.cumsum(jax.nn.softmax(hgrn_lb_logits.astype(F32), axis=0), axis=0)
    for l in range(DEPTH):
        h = rms_norm(x, norm_mix[l])
        j = l // 2
        if l % 2 == 0:
            mix = retention_hgrn2_mixer(h, w_in_ab[j], w_out_ab[j], ret_gnorm[j], lb_table[l],
                                        hgrn_onorm[j], cos_r, sin_r)
        else:
            mix = stickbreak_diff_mixer(h, w_in_cd[j], w_out_cd[j], diff_qnorm[j], diff_knorm[j],
                                        diff_lam_q1[j], diff_lam_k1[j], diff_lam_q2[j], diff_lam_k2[j],
                                        diff_subln[j], cos_d, sin_d, l)
        x = x + mix.astype(x.dtype)
        h = rms_norm(x, norm_ffn[l])
        x = x + hierarchical_moe(h, router_group_w[l], router_group_b[l], router_expert_w[l],
                                 router_expert_b[l], w_gate[l], w_up[l], w_down[l]).astype(x.dtype)
    return x


_drawn_inputs = setup_inputs


def setup_inputs(seed=0):
    import zlib

    import numpy as np

    out = dict(_drawn_inputs(seed))
    spreads = {}
    factors = {'hgrn_lb_logits': 2.792,
     'diff_qnorm': 4.685,
     'diff_knorm': 6.85,
     'diff_lam_k1': 3.028,
     'diff_lam_k2': 2.721,
     'diff_subln': 4.081,
     'router_group_b': 3.179}
    for name, (base, spread) in spreads.items():
        noise = np.random.default_rng([zlib.crc32(name.encode()), seed]).standard_normal(out[name].shape)
        drawn = base * np.exp(spread * noise) if base else spread * noise
        out[name] = jnp.asarray(drawn.astype(out[name].dtype))
    for name, factor in factors.items():
        out[name] = (out[name] * factor).astype(out[name].dtype)
    return out
```

```python
from contextlib import ExitStack
import math

import numpy as np
import concourse.bass as bass
from concourse import mybir

ALU = mybir.AluOpType
ACT = mybir.ActivationFunctionType
F32 = mybir.dt.float32
I32 = mybir.dt.int32
AX = mybir.AxisListType.X

P = 128
SEQ = 256
D = 1024
TC = SEQ // P
KC = D // P
HEADS = 4
HD = 128
GROUP_W = HEADS * HD
EPS = 1e-6
SUB = 16
NSUB = SEQ // SUB
N_GROUPS = 4
PER_GROUP = 8
N_EXPERTS = N_GROUPS * PER_GROUP
FF = 512
FC = FF // P
SLOTS = 64
PAIRS = N_EXPERTS // 2
OVER_ROUNDS = SEQ // SLOTS - 1
N_SMALL = 20
RING = 6
UNIT = 4096
UNITS_IN = (8, 6)
UNITS_OUT = 2
UNITS_PAIR = 6
BIG = 1e30
LAM_INIT = 0.8 - 0.6 * math.exp(-0.3 * 1)
TWO_PI_HI = 6.28125
TWO_PI_LO = 2 * math.pi - 6.28125
ROUND = 1.5 * 2.0 ** 23
F_FLOOR = math.exp(-10.0)
SCALE = HD ** -0.5
SCALE_DIFF = 64 ** -0.5
TRI = 384

BLOCKS = ((5, 4, 0, 1, 2, 6, 3, 7), (0, 1, 2, 3, 4, 5))
TURNED = ((5, 4), (0, 1))

ROOTS = ((2, 2), (20, 8), (28, 8), (2, 2), (2, 2), (44, 16), (44, 16), (44, 8), (2, 2))


def shape_constants():
    p = np.arange(P)[:, None]
    f128, f256 = np.arange(P)[None, :], np.arange(SEQ)[None, :]
    parts = {}
    parts["ident"] = (p == f128)
    parts["before"] = (p < f128)
    parts["from_on"] = (p >= f128)
    parts["ones"] = np.ones((P, SEQ))
    parts["iota"] = np.broadcast_to(np.arange(SLOTS)[None, :], (P, SLOTS))
    parts["falling"] = np.broadcast_to((N_EXPERTS - np.arange(N_EXPERTS))[None, :], (P, N_EXPERTS))
    le = np.concatenate([p <= f256, p <= f128], 1)
    lt = np.concatenate([p < f256, p < f128], 1)
    rel = np.concatenate([f256 - p, f128 - p], 1).astype(np.float64)
    parts["decay"] = np.concatenate(
        [np.where(rel >= 0, (1 - 2.0 ** (-5 - h)) ** np.maximum(rel, 0), 0.0) * SCALE for h in range(HEADS)], 1)
    parts["causal_scale"] = le * SCALE
    parts["strict"] = lt
    parts["strict_add"] = np.where(lt, 0.0, -BIG)
    low = p >= f128
    parts["causal_add"] = np.where(np.concatenate([low, np.ones((P, P), bool), low], 1), 0.0, -BIG)
    inv = [1.0 / (np.float32(10000.0) ** (np.arange(0, d, 2, dtype=np.float32) / np.float32(d))) for d in (128, 64)]
    parts["inv_freq"] = np.broadcast_to(np.concatenate(inv)[None, :], (P, 96))
    where, at = {}, 0
    for name, a in parts.items():
        where[name] = (at, at + a.shape[1])
        at += a.shape[1]
    return np.ascontiguousarray(np.concatenate([a.astype(np.float32) for a in parts.values()], 1)), where


class InTurn:

    def __init__(self, eng, sem, base=0):
        self.eng, self.sem, self.base, self.n = eng, sem, base, 0

    def __call__(self, instruction):
        self.n += 1
        instruction.then_inc(self.sem, 1)
        self.eng.wait_ge(self.sem, self.base + self.n)


def build(nc, t, where, const_width, stop_after=4):
    with ExitStack() as ctx:
        def sb(name, shape, dt=F32):
            return ctx.enter_context(nc.sbuf_tensor(name, shape, dt))

        def sem(name):
            return ctx.enter_context(nc.semaphore(name))

        ring = sb("ring", [P, RING, UNIT])
        consts = sb("consts", [P, const_width])
        x = sb("x", [P, TC, D])
        h = sb("h", [P, TC, KC, P])
        hT = sb("hT", [P, KC, SEQ])
        mixed = sb("mixed", [P, TC, D])
        gain = sb("gain", [P, D])
        small = sb("small", [P, 96])
        pos_i = sb("pos_i", [P, TC], I32)
        rope = sb("rope", [P, 2, TC, 96])
        psum = ctx.enter_context(nc.psum_tensor("psum", [P, 8, 512], F32))

        def const(name):
            return consts[:, where[name][0]:where[name][1]]

        ident, before, from_on = const("ident"), const("before"), const("from_on")
        ones = const("ones")
        sin_t, cos_t = rope[:, 0], rope[:, 1]

        arena_w = 12416
        arena = sb("arena", [P, arena_w])
        taken = {}

        def part(who, width, shape=None, **dims):
            a = taken.get(who, 0)
            taken[who] = a + width
            assert taken[who] <= arena_w, (who, taken)
            v = arena[:, a:a + width]
            return v.rearrange(shape, **dims) if shape else v

        qT = part("mix", 1024, "p (h t) -> p h t", h=HEADS)
        kT = part("mix", 1024, "p (h t) -> p h t", h=HEADS)
        q2T = part("mix", 1024, "p (h t) -> p h t", h=HEADS)
        k2T = part("mix", 1024, "p (h t) -> p h t", h=HEADS)
        val = part("mix", 1024, "p (c n) -> p c n", c=TC)
        val2 = part("mix", 1024, "p (c n) -> p c n", c=TC)
        st = part("mix", 2 * TRI, "p (b n) -> p b n", b=2)
        keep_mix = taken["mix"]
        cumf = part("mix", 1024, "p (h t) -> p h t", h=HEADS)
        tmp = part("mix", 1024)
        st2 = part("mix", HEADS * TRI, "p (h n) -> p h n", h=HEADS)
        ke0 = h[:, :, :, :].rearrange("p a b s -> p (a b) s")
        ke1 = part("mix", NSUB // 2 * P, "p (i s) -> p i s", s=P)
        taken["mix1"] = keep_mix
        h_flat = h[:, :, :, :].rearrange("p a b s -> p (a b s)")
        sta = h_flat[:, 0:HEADS * TRI].rearrange("p (h n) -> p h n", h=HEADS)
        sbe = h_flat[:, HEADS * TRI:(HEADS + 1) * TRI]
        sbz = part("mix1", 2 * TRI, "p (b n) -> p b n", b=2)
        sbl = part("mix1", TRI)
        dss = part("mix1", 4 * TRI, "p (b c n) -> p b c n", b=2, c=2)
        dff = part("mix1", 2 * TRI, "p (b n) -> p b n", b=2)
        tmp1 = part("mix1", 1024)
        tmp2 = part("mix1", 1024)
        xT = part("moe", KC * P, "p (c s) -> p c s", c=KC)
        sel = part("moe", TC * P, "p (c s) -> p c s", c=TC)
        selw = part("moe", TC * P, "p (c s) -> p c s", c=TC)
        spread = part("moe", TC * P, "p (c t) -> p c t", c=TC)
        eneg = part("moe", FF)
        act_h = part("moe", FF, "p (c s) -> p c s", c=FC)
        actT = part("moe", FC * P, "p (c s) -> p c s", c=FC)
        y_sb = part("moe", D)
        rt = part("moe", 2048)
        rank = part("moe", TC * (N_EXPERTS + 2), "p (c e) -> p c e", c=TC)
        wtab = part("moe", TC * (N_EXPERTS + 2), "p (c e) -> p c e", c=TC)
        picked = part("moe", TC * N_EXPERTS, "p (c e) -> p c e", c=TC)
        rw = sb("rw", [P, 2, KC, 36])
        rb = sb("rb", [P, 2, 36])
        lbt = sb("lbt", [P, 3, HEADS])
        lbw = sb("lbw", [P, 4, HEADS])
        retg = sb("retg", [P, 2, GROUP_W])
        dg = sb("dg", [P, 2, 64])
        dlam = sb("dlam", [P, 4, 64])
        subln = sb("subln", [P, HD])
        over_i = sb("over_i", [P, 2], I32)

        names = ["small_landed", "x_landed", "gain_landed", "gain_used", "unit_used", "stored",
                 "act_turn", "dve_turn", "rope_args", "rope_ready", "zeroed", "pos_ready",
                 "squares", "normed", "h_turned", "hT_ready", "lb_in", "lb_exp",
                 "f_exp", "f_ready", "f_log", "cum_ready", "q_exp", "mid_in", "mid_exp", "qe_ready",
                 "ke_exp", "ke_ready", "scores_done", "st_ready", "pv_done", "sq_out", "out_used",
                 "roped", "turned", "turned_sb", "val_ready", "gate_exp", "gated", "mix_turned", "mixT_ready",
                 "added", "finished", "finished_first",
                 "stick_abs", "stick_log", "stick_l", "stick_r", "stick_arg", "stick_a",
                 "diff_in", "diff_max", "diff_exp", "diff_a", "diff_turned", "diff_aT", "lam_dot", "lam_exp",
                 "logits_done", "group_max", "group_exp", "top_diff", "top_exp", "picked_ready", "ranks_done",
                 "route_ready", "norm_sq", "root_in", "root_out"]
        S = {n: sem(n) for n in names}
        proj_used = [sem(f"proj_used{i}") for i in range(2)]
        landed = [sem(f"landed{i}") for i in range(RING)]
        over_landed = {(l, i): sem(f"over{l}_landed{i}") for l in range(2) for i in range(RING)}
        MOE_NAMES = ["sel_ready", "gathered", "xT_ready", "exp_ready", "act_ready",
                     "turned", "actT_ready", "y_ready", "spread_done", "round_done", "added",
                     "turn", "used"]
        M = {l: {n: sem(f"moe{l}_{n}") for n in MOE_NAMES} for l in range(2)}

        block = ctx.enter_context(nc.Block())

        def unit_base(layer):
            return layer * (UNITS_IN[0] + UNITS_OUT + UNITS_PAIR * PAIRS)

        def moe_base(layer):
            return unit_base(layer) + UNITS_IN[layer] + UNITS_OUT

        def wait_unit(eng, u):
            eng.wait_ge(landed[u % RING], 16 * (u // RING + 1))

        def and_wait(eng, instruction, signal, value):
            instruction.then_inc(signal, 1)
            eng.wait_ge(signal, value)

        def proj(g):
            return psum[:, 2 * (g % 2):2 * (g % 2) + 2, :]

        def wait_projected(eng, n):
            eng.wait_ge(S["unit_used"], n if n <= UNITS_IN[0] else unit_base(1) + n - UNITS_IN[0])

        def flat(a):
            return a.rearrange("p a b -> p (a b)")

        def heads(a):
            return a.rearrange("p c (h d) -> p c h d", h=HEADS)

        @block.sync
        def _(sp):
            w_in = (t["w_in_ab"], t["w_in_cd"])
            w_out = (t["w_out_ab"], t["w_out_cd"])

            def load_unit(u, dst_cols, src):
                if u >= RING:
                    sp.wait_ge(S["unit_used"], u - RING + 1)
                sp.dma_start(dst_cols(ring[:, u % RING, :]), src).then_inc(landed[u % RING], 16)

            def pair_units(layer, pair):
                for w, rows in (("w_gate", KC), ("w_up", KC), ("w_down", FC)):
                    for e in range(2):
                        yield t[w][layer, bass.ds(2 * pair + e, 1)].rearrange("a (p c) n -> p (a c n)", c=rows)

            sp.dma_start(x[:, :, :], t["x"].rearrange("b (c p) d -> p (b c) d", p=P)).then_inc(S["x_landed"], 16)
            sp.dma_start(consts[:, :], t["consts"]).then_inc(S["small_landed"], 16)
            sp.dma_start(gain[:, :], t["norm_mix"][0:1, :].broadcast_to([P, D])).then_inc(S["gain_landed"], 16)

            def load_in(layer, n):
                b = BLOCKS[layer][n]
                src = w_in[layer][0].rearrange("(p c) n -> p c n", c=KC)[:, :, b * 512:(b + 1) * 512]
                load_unit(unit_base(layer) + n, lambda s: s.rearrange("p (c n) -> p c n", c=KC), src)

            for n in range(2):
                load_in(0, n)
            with nc.allow_non_contiguous_dma("small tables"):
                small_loads = [
                    (pos_i[:, :], t["positions"].rearrange("b (c p) -> p (b c)", p=P)),
                    (lbt[:, :, :], t["hgrn_lb_logits"].rearrange("r (h p) -> p r h", p=P)),
                    (retg[:, 0, :], t["ret_gnorm"].rearrange("a h d -> a (h d)").broadcast_to([P, GROUP_W])),
                    (retg[:, 1, :], t["hgrn_onorm"].rearrange("a h d -> a (h d)").broadcast_to([P, GROUP_W])),
                    (dg[:, 0, :], t["diff_qnorm"].broadcast_to([P, 64])),
                    (dg[:, 1, :], t["diff_knorm"].broadcast_to([P, 64])),
                    (dlam[:, 0, :], t["diff_lam_q1"].broadcast_to([P, 64])),
                    (dlam[:, 1, :], t["diff_lam_k1"].broadcast_to([P, 64])),
                    (dlam[:, 2, :], t["diff_lam_q2"].broadcast_to([P, 64])),
                    (dlam[:, 3, :], t["diff_lam_k2"].broadcast_to([P, 64])),
                    (subln[:, :], t["diff_subln"].broadcast_to([P, HD])),
                ]
                for l in range(2):
                    small_loads.append((rw[:, l, :, 0:4], t["router_group_w"][l].rearrange("(p c) n -> p c n", c=KC)))
                    small_loads.append((rw[:, l, :, 4:36], t["router_expert_w"][l].rearrange("(p c) n -> p c n", c=KC)))
                    small_loads.append((rb[:, l, 0:4], t["router_group_b"][l:l + 1, :].broadcast_to([P, 4])))
                    small_loads.append((rb[:, l, 4:36], t["router_expert_b"][l:l + 1, :].broadcast_to([P, 32])))
                for dst, src in small_loads:
                    sp.dma_start(dst, src).then_inc(S["small_landed"], 16)
            assert len(small_loads) + 1 == N_SMALL

            for layer in range(2):
                base = unit_base(layer)
                for n in range(2 if layer == 0 else 0, UNITS_IN[layer]):
                    load_in(layer, n)
                sp.wait_ge(S["gain_used"], 2 * layer + 1)
                sp.dma_start(gain[:, :], t["norm_ffn"][layer:layer + 1, :].broadcast_to([P, D])).then_inc(S["gain_landed"], 16)
                for n in range(UNITS_OUT):
                    src = w_out[layer][0, 512 * n:512 * (n + 1), :].rearrange("(c p) n -> p c n", p=P)
                    load_unit(base + UNITS_IN[layer] + n, lambda s: s.rearrange("p (c n) -> p c n", c=4), src)
                mb = moe_base(layer)
                with sp.Fori(0, PAIRS) as i:
                    for j, src in enumerate(pair_units(layer, i)):
                        sp.wait_ge(S["unit_used"], i * UNITS_PAIR + (mb + 2 * (j // 2) + 2 - RING))
                        sp.dma_start(ring[:, (mb + j) % RING, :], src).then_inc(landed[(mb + j) % RING], 16)
                sp.wait_ge(S["route_ready"], layer + 1)
                count = sp.value_load(over_i[0:1, layer:layer + 1], min_val=0, max_val=SEQ)
                with sp.If(count > SLOTS):
                    sp.wait_ge(S["unit_used"], mb + UNITS_PAIR * PAIRS)
                    m = M[layer]
                    for j, src in enumerate(pair_units(layer, 0)):
                        sp.dma_start(ring[:, j, :], src).then_inc(over_landed[layer, j], 16)

                    def over_pair(n, pair):
                        for j, src in enumerate(pair_units(layer, pair)):
                            sp.wait_ge(m["used"], (n - 1) * UNITS_PAIR + (2 * (j // 2) + 2))
                            sp.dma_start(ring[:, j, :], src).then_inc(over_landed[layer, j], 16)

                    with sp.Fori(1, PAIRS) as i:
                        over_pair(i, i)
                    with sp.Fori(1, OVER_ROUNDS) as r:
                        with sp.Fori(0, PAIRS) as i:
                            over_pair(r * PAIRS + i, i)
                    sp.wait_ge(m["used"], OVER_ROUNDS * PAIRS * UNITS_PAIR)
                with sp.Else():
                    sp.nop()
                if layer == 0:
                    sp.wait_ge(S["gain_used"], 2)
                    sp.dma_start(gain[:, :], t["norm_mix"][1:2, :].broadcast_to([P, D])).then_inc(S["gain_landed"], 16)
            sp.wait_ge(S["finished"], 1)
            sp.dma_start(t["out"].rearrange("b (c p) d -> p (b c) d", p=P), x[:, :, :]).then_inc(S["stored"], 16)
            sp.wait_ge(S["stored"], 16)

        ACC, GATE, UP, YB = 0, 4, 5, 6

        def wait_pair(eng, layer, rnd, i, units):
            if isinstance(rnd, int):
                eng.wait_ge(S["unit_used"], i * UNITS_PAIR + (moe_base(layer) + units))
            else:
                eng.wait_ge(M[layer]["used"], (rnd - 1) * (PAIRS * UNITS_PAIR) + i * UNITS_PAIR + units)

        def moe_pe(pe, layer, over, rnd):
            m = M[layer]
            n17, n16 = rnd * (PAIRS + 1), rnd * PAIRS
            mb = moe_base(layer)

            def gather():
                for c in range(KC):
                    for tc in range(TC):
                        mm = pe.matmul(psum[:, YB + c // 4, (c % 4) * P:(c % 4 + 1) * P], h[:, tc, c, :],
                                       sel[:, tc, :], start=tc == 0, stop=tc == TC - 1)
                mm.then_inc(m["gathered"], 1)

            def spread_back():
                for tc in range(TC):
                    for n in range(2):
                        mm = pe.matmul(psum[:, ACC + 2 * tc + n, :], spread[:, tc, :],
                                       y_sb[:, 512 * n:512 * (n + 1)], start=False, stop=False,
                                       skip_group_check=True)
                mm.then_inc(m["spread_done"], 1)

            def unit(i, j):
                if over:
                    pe.wait_ge(over_landed[layer, j], ((rnd - 1) * PAIRS + i + 1) * 16)
                    return ring[:, j, :]
                u = mb + j
                pe.wait_ge(landed[u % RING], i * 16 + 16 * (u // RING + 1))
                return ring[:, u % RING, :]

            used = m["used"] if over else S["unit_used"]
            pe.wait_ge(m["y_ready"], 2 * (n17 + 1))
            for b in range(4):
                pe.matmul(psum[:, ACC + b, :], spread[:, 0, :], y_sb[:, 0:512], start=True, stop=False,
                          skip_group_check=True)
            pe.wait_ge(m["sel_ready"], n17 + 1)
            gather()
            with pe.Fori(0, PAIRS) as i:
                pe.wait_ge(m["xT_ready"], n17 + i + 1)
                for bank, w in ((GATE, 0), (UP, 2)):
                    wa = unit(i, w).rearrange("p (c n) -> p c n", c=KC)
                    wb = unit(i, w + 1).rearrange("p (c n) -> p c n", c=KC)
                    for c in range(KC):
                        pe.matmul(psum[0:SLOTS, bank, :], xT[:, c, 0:SLOTS], wa[:, c, :],
                                       start=c == 0, stop=c == KC - 1)
                        mm = pe.matmul(psum[SLOTS:P, bank, :], xT[:, c, SLOTS:P], wb[:, c, :],
                                       start=c == 0, stop=c == KC - 1)
                    mm.then_inc(used, 2)
                pe.wait_ge(m["y_ready"], 2 * (n17 + i + 1))
                spread_back()
                pe.wait_ge(m["sel_ready"], n17 + i + 2)
                gather()
                pe.wait_ge(m["act_ready"], n16 + i + 1)
                for c in range(FC):
                    pe.transpose(psum[:, GATE, c * P:(c + 1) * P], act_h[:, c, :], ident)
                for tc in range(TC):
                    mm = pe.transpose(psum[:, UP, tc * P:(tc + 1) * P], selw[:, tc, :], ident)
                mm.then_inc(m["turned"], 1)
                pe.wait_ge(m["actT_ready"], n16 + i + 1)
                pe.wait_ge(m["xT_ready"], n17 + i + 2)
                wa = unit(i, 4).rearrange("p (c n) -> p c n", c=FC)
                wb = unit(i, 5).rearrange("p (c n) -> p c n", c=FC)
                for n in range(2):
                    for c in range(FC):
                        pe.matmul(psum[0:SLOTS, YB + n, :], actT[:, c, 0:SLOTS],
                                       wa[:, c, 512 * n:512 * (n + 1)], start=c == 0, stop=c == FC - 1)
                        mm = pe.matmul(psum[SLOTS:P, YB + n, :], actT[:, c, SLOTS:P],
                                       wb[:, c, 512 * n:512 * (n + 1)], start=c == 0, stop=c == FC - 1)
                mm.then_inc(used, 2)
            pe.wait_ge(m["y_ready"], 2 * (n17 + PAIRS + 1))
            spread_back()

        def moe_act(act, layer, over, rnd):
            m = M[layer]
            n17, n16 = rnd * (PAIRS + 1), rnd * PAIRS

            def keep_gathered():
                nc.scalar.copy(xT, psum[:, YB:YB + 2, :].rearrange("p b (c s) -> p (b c) s", s=P)).then_inc(m["xT_ready"], 1)

            act.wait_ge(m["gathered"], n17 + 1)
            keep_gathered()
            with act.Fori(0, PAIRS) as i:
                wait_pair(act, layer, rnd, i, 2)
                nc.scalar.activation(eneg, psum[:, GATE, :], ACT.Exp, scale=-1.0).then_inc(m["exp_ready"], 1)
                act.wait_ge(m["gathered"], n17 + i + 2)
                keep_gathered()
                act.wait_ge(m["turned"], n16 + i + 1)
                nc.scalar.copy(actT, psum[:, GATE, :].rearrange("p (c s) -> p c s", c=FC))
                nc.scalar.copy(spread, psum[:, UP, 0:TC * P].rearrange("p (c s) -> p c s", c=TC)).then_inc(m["actT_ready"], 1)
                wait_pair(act, layer, rnd, i, 6)
                nc.scalar.copy(y_sb[:, 0:512], psum[:, YB, :]).then_inc(m["y_ready"], 1)

        def moe_dve(dve, layer, over, rnd):
            m = M[layer]
            n17, n16 = rnd * (PAIRS + 1), rnd * PAIRS
            STEPS = 3

            def one_hots(pair):
                for e in range(2):
                    for tc in range(TC):
                        r = nc.vector.tensor_scalar(sel[:, tc, e * SLOTS:(e + 1) * SLOTS], const("iota"),
                                                    rank[:, tc, bass.ds(pair * 2 + e, 1)], None, ALU.is_equal)
                r.then_inc(m["sel_ready"], 1)

            def weighted(pair):
                for e in range(2):
                    for tc in range(TC):
                        r = nc.vector.tensor_scalar(selw[:, tc, e * SLOTS:(e + 1) * SLOTS], const("iota"),
                                                    rank[:, tc, bass.ds(pair * 2 + e, 1)],
                                                    wtab[:, tc, bass.ds(pair * 2 + e, 1)], ALU.is_equal, ALU.mult)
                return r

            nc.vector.memset(y_sb, 0.0).then_inc(m["y_ready"], 1)
            nc.vector.memset(flat(spread), 0.0).then_inc(m["y_ready"], 1)
            one_hots(0)
            weighted(0)
            with dve.Fori(0, PAIRS) as i:
                turn = InTurn(dve, m["turn"], (n16 + i) * STEPS)
                dve.wait_ge(m["gathered"], n17 + i + 1)
                one_hots(i + 1)
                dve.wait_ge(m["exp_ready"], n16 + i + 1)
                turn(nc.vector.tensor_scalar(eneg, eneg, 1.0, None, ALU.add))
                turn(nc.vector.reciprocal(eneg, eneg))
                turn(nc.vector.tensor_tensor(eneg, psum[:, GATE, :], eneg, ALU.mult))
                assert turn.n == STEPS
                wait_pair(dve, layer, rnd, i, 4)
                nc.vector.tensor_tensor(act_h.rearrange("p c s -> p s c"), psum[:, UP, :].rearrange("p (s c) -> p s c", c=FC),
                                        eneg.rearrange("p (s c) -> p s c", c=FC), ALU.mult).then_inc(m["act_ready"], 1)
                dve.wait_ge(m["turned"], n16 + i + 1)
                weighted(i + 1)
                wait_pair(dve, layer, rnd, i, 6)
                nc.vector.tensor_copy(y_sb[:, 512:1024], psum[:, YB + 1, :]).then_inc(m["y_ready"], 1)
            dve.wait_ge(m["spread_done"], n17 + PAIRS + 1)
            for tc in range(TC):
                r = nc.vector.tensor_tensor(x[:, tc, :], x[:, tc, :], flat(psum[:, 2 * tc:2 * tc + 2, :]), ALU.add)
            and_wait(dve, r, m["added"], rnd + 1)

        roots_asked, roots_taken = [], []

        def inverse_root(dve, instruction, turn, col, count):
            assert ROOTS[len(roots_asked)] == (col, count)
            roots_asked.append((col, count))
            instruction.then_inc(S["root_in"], 1)
            dve.wait_ge(S["root_out"], len(roots_asked))
            v, y, z = small[:, col:col + count], small[:, 64:64 + count], small[:, 80:80 + count]
            turn(nc.vector.tensor_tensor(z, y, y, ALU.mult))
            turn(nc.vector.tensor_tensor(z, z, v, ALU.mult))
            turn(nc.vector.tensor_scalar(z, z, -0.5, 1.5, ALU.mult, ALU.add))
            turn(nc.vector.tensor_tensor(v, y, z, ALU.mult))

        def take_root(act, turn):
            col, count = ROOTS[len(roots_taken)]
            roots_taken.append(col)
            act.wait_ge(S["root_in"], len(roots_taken))
            y = small[:, 64:64 + count]
            turn(nc.scalar.activation(y, small[:, col:col + count], ACT.Ln))
            nc.scalar.activation(y, y, ACT.Exp, scale=-0.5).then_inc(S["root_out"], 1)

        def norm_act(act, turn, n):
            for tc in range(TC):
                nc.scalar.activation(mixed[:, tc, :], x[:, tc, :], ACT.Square,
                                     accum_out=small[:, tc:tc + 1]).then_inc(S["squares"], 1)
            take_root(act, turn)

        def norm_dve(dve, turn, n):
            dve.wait_ge(S["squares"], TC * (n + 1))
            inverse_root(dve, nc.vector.tensor_scalar(small[:, 2:4], small[:, 0:2], 1.0 / D, EPS, ALU.mult, ALU.add), turn, 2, 2)
            dve.wait_ge(S["gain_landed"], 16 * (n + 1))
            for tc in range(TC):
                nc.vector.scalar_tensor_tensor(
                    h[:, tc].rearrange("p c q -> p q c"), x[:, tc, :].rearrange("p (q c) -> p q c", c=KC),
                    small[:, 2 + tc:3 + tc], gain[:, :].rearrange("p (q c) -> p q c", c=KC), ALU.mult, ALU.mult).then_inc(S["normed"], 1)
            dve.wait_ge(S["normed"], TC * (n + 1))
            nc.vector.memset(small[:, 4:5], 0.0).then_inc(S["gain_used"], 1)

        def turn_h(pe, n):
            for tc in range(TC):
                pe.wait_ge(S["normed"], TC * n + tc + 1)
                for c in range(KC):
                    mm = pe.transpose(psum[:, c // 2, (c % 2) * SEQ + tc * P:(c % 2) * SEQ + (tc + 1) * P],
                                      h[:, tc, c, :], ident)
            mm.then_inc(S["h_turned"], 1)

        def turn_mixed(pe):
            for tc in range(TC):
                for c in range(KC):
                    mm = pe.transpose(psum[:, c // 2, (c % 2) * SEQ + tc * P:(c % 2) * SEQ + (tc + 1) * P],
                                      mixed[:, tc, c * P:(c + 1) * P], ident)
            mm.then_inc(S["mix_turned"], 1)

        def keep_hT(half, copy):
            return copy(hT[:, 4 * half:4 * half + 4, :].rearrange("p (b c) t -> p b (c t)", b=2),
                        psum[:, 2 * half:2 * half + 2, :])

        @block.tensor
        def _(pe):
            def project(layer, n):
                g = (0, UNITS_IN[0])[layer] + n
                u = unit_base(layer) + n
                wait_unit(pe, u)
                if g >= 2:
                    pe.wait_ge(proj_used[g % 2], g // 2)
                w = ring[:, u % RING, :].rearrange("p (c n) -> p c n", c=KC)
                banks = proj(g)
                if BLOCKS[layer][n] in TURNED[layer]:
                    for m in range(HEADS):
                        for c in range(KC):
                            mm = pe.matmul(banks[:, m // 2, (m % 2) * SEQ:(m % 2 + 1) * SEQ],
                                           w[:, c, m * P:(m + 1) * P], hT[:, c, :], start=c == 0, stop=c == KC - 1)
                else:
                    for tc in range(TC):
                        for c in range(KC):
                            mm = pe.matmul(banks[:, tc, :], hT[:, c, tc * P:(tc + 1) * P], w[:, c, :],
                                           start=c == 0, stop=c == KC - 1)
                mm.then_inc(S["unit_used"], 1)

            def causal(bank, q, k):
                pe.matmul(psum[:, bank, 0:SEQ], k[:, 0:P], q, start=True, stop=True)
                return pe.matmul(psum[:, bank, SEQ:TRI], k[:, P:SEQ], q[:, P:SEQ], start=True, stop=True)

            def attend(bank, hd, s, v):
                cols = slice(hd * HD, (hd + 1) * HD)
                pe.matmul(psum[:, bank, cols], s[:, 0:P], v[:, 0, cols], start=True, stop=True)
                pe.matmul(psum[:, bank + 1, cols], s[:, P:SEQ], v[:, 0, cols], start=True, stop=False)
                mm = pe.matmul(psum[:, bank + 1, cols], s[:, SEQ:TRI], v[:, 1, cols], start=False, stop=True)
                mm.then_inc(S["pv_done"], 1)

            def turn_roped(col):
                for hd in range(HEADS):
                    for tc in range(TC):
                        mm = pe.transpose(psum[:, 6 + hd // 2, (hd % 2) * SEQ + tc * P:(hd % 2) * SEQ + (tc + 1) * P],
                                          mixed[:, tc, col + hd * HD:col + (hd + 1) * HD], ident)
                mm.then_inc(S["turned"], 1)

            def project_out(layer):
                pe.wait_ge(S["gated"], 2 * (layer + 1))
                for g in range(2):
                    pe.wait_ge(proj_used[g], (4, 7)[layer])
                turn_mixed(pe)
                pe.wait_ge(S["mixT_ready"], 2 * (layer + 1))
                for un in range(UNITS_OUT):
                    u = unit_base(layer) + UNITS_IN[layer] + un
                    wait_unit(pe, u)
                    w = ring[:, u % RING, :].rearrange("p (c n) -> p c n", c=4)
                    for c in range(4):
                        for tc in range(TC):
                            for n in range(2):
                                mm = pe.matmul(psum[:, 4 + 2 * tc + n, :], hT[:, 4 * un + c, tc * P:(tc + 1) * P],
                                               w[:, c, 512 * n:512 * (n + 1)], start=un == 0 and c == 0,
                                               stop=un == 1 and c == 3)
                    mm.then_inc(S["unit_used"], 1)

            def route_and_experts(layer):
                n = 2 * layer + 1
                turn_h(pe, n)
                pe.wait_ge(S["hT_ready"], 2 * (n + 1))
                pe.wait_ge(S["small_landed"], 16 * N_SMALL)
                for tc in range(TC):
                    for c in range(KC):
                        mm = pe.matmul(psum[:, 4, tc * 36:(tc + 1) * 36], hT[:, c, tc * P:(tc + 1) * P],
                                       rw[:, layer, c, :], start=c == 0, stop=c == KC - 1)
                mm.then_inc(S["logits_done"], 1)
                pe.wait_ge(S["picked_ready"], layer + 1)
                pe.matmul(psum[:, 5, 0:32], before, picked[:, 0, :], start=True, stop=True)
                pe.matmul(psum[:, 5, 32:64], before, picked[:, 1, :], start=True, stop=False)
                pe.matmul(psum[:, 5, 32:64], ones[:, 0:P], picked[:, 0, :], start=False, stop=True)
                pe.matmul(psum[:, 5, 64:96], ones[:, 0:P], picked[:, 0, :], start=True, stop=False)
                mm = pe.matmul(psum[:, 5, 64:96], ones[:, 0:P], picked[:, 1, :], start=False, stop=True)
                mm.then_inc(S["ranks_done"], 1)
                moe_pe(pe, layer, 0, 0)
                with pe.If(pe.value_load(over_i[0:1, layer:layer + 1], min_val=0, max_val=SEQ) > SLOTS):
                    with pe.Fori(0, OVER_ROUNDS) as r:
                        moe_pe(pe, layer, 1, r + 1)
                with pe.Else():
                    pe.nop()

            pe.wait_ge(S["small_landed"], 16 * N_SMALL)
            turn_h(pe, 0)
            pe.wait_ge(S["hT_ready"], 2)
            k = 0

            def next_scores():
                nonlocal k
                if k >= 2:
                    pe.wait_ge(S["st_ready"], k - 1)
                k += 1
                return 4 + (k - 1) % 2

            def scores_hgrn(hd):
                pe.wait_ge(S["qe_ready"], 1)
                pe.wait_ge(S["ke_ready"], 2 * (hd + 1))
                bank = next_scores()
                for i in range(NSUB):
                    q = q2T[:, hd, i * SUB:(i + 1) * SUB]
                    mm = pe.matmul(psum[:, bank, i * SUB:(i + 1) * SUB], ke0[:, i, :], q, start=True, stop=True)
                    if i >= NSUB // 2:
                        mm = pe.matmul(psum[:, bank, SEQ - P + i * SUB:SEQ - P + (i + 1) * SUB], ke1[:, i - NSUB // 2, :], q,
                                       start=True, stop=True)
                mm.then_inc(S["scores_done"], 1)

            def scores_ret(hd):
                bank = next_scores()
                causal(bank, qT[:, hd, :], kT[:, hd, :]).then_inc(S["scores_done"], 1)

            for n in range(4):
                project(0, n)
            scores_hgrn(0)
            project(0, 4)
            pe.wait_ge(S["roped"], 1)
            turn_roped(0)
            pe.wait_ge(S["turned_sb"], 1)
            pe.wait_ge(S["roped"], 2)
            turn_roped(GROUP_W)
            scores_hgrn(1)
            project(0, 5)
            pe.wait_ge(S["turned_sb"], 2)
            pe.wait_ge(S["val_ready"], 1)
            scores_ret(0)
            scores_ret(1)
            for hd in range(HEADS):
                pe.wait_ge(S["st_ready"], 2 + hd + 1)
                attend(6, hd, st[:, hd % 2, :], val)
                if hd + 2 < HEADS:
                    scores_ret(hd + 2)
            scores_hgrn(2)
            project(0, 6)
            scores_hgrn(3)
            project(0, 7)
            pe.wait_ge(S["val_ready"], 2)
            pe.wait_ge(S["out_used"], 1)
            pe.wait_ge(S["st_ready"], 8)
            for hd in range(HEADS):
                attend(6, hd, st2[:, hd, :], val2)
            project_out(0)
            route_and_experts(0)

            turn_h(pe, 2)
            pe.wait_ge(S["hT_ready"], 6)

            def stick_scores(hd):
                if hd >= 1:
                    pe.wait_ge(S["stick_abs"], hd)
                else:
                    pe.wait_ge(S["turned_sb"], 4)
                causal(4, qT[:, hd, :], kT[:, hd, :]).then_inc(S["scores_done"], 1)

            def stick_sums(hd):
                pe.wait_ge(S["stick_l"], hd + 1)
                if hd >= 1:
                    pe.wait_ge(S["stick_arg"], hd)
                pe.matmul(psum[:, 5, 0:SEQ], from_on, sbl[:, 0:SEQ], start=True, stop=False, skip_group_check=True)
                pe.matmul(psum[:, 5, P:SEQ], ones[:, 0:P], sbl[:, SEQ:TRI], start=False, stop=True, skip_group_check=True)
                mm = pe.matmul(psum[:, 5, SEQ:TRI], from_on, sbl[:, SEQ:TRI], start=True, stop=True, skip_group_check=True)
                mm.then_inc(S["stick_r"], 1)

            project(1, 0)
            project(1, 1)
            stick_scores(0)
            for hd in range(HEADS):
                project(1, 2 + hd)
                stick_sums(hd)
                if hd + 1 < HEADS:
                    stick_scores(hd + 1)
            pe.wait_ge(S["roped"], 3)
            turn_roped(0)
            pe.wait_ge(S["turned_sb"], 5)
            pe.wait_ge(S["roped"], 4)
            turn_roped(GROUP_W)
            pe.wait_ge(S["turned_sb"], 6)
            pe.wait_ge(S["val_ready"], 4)
            pe.wait_ge(S["stick_a"], HEADS)
            for hd in range(HEADS):
                attend(6, hd, sta[:, hd, :], val)

            def diff_scores(hd):
                if hd >= 1:
                    pe.wait_ge(S["diff_in"], hd)
                for part_ in range(2):
                    rows = slice(64 * part_, 64 * part_ + 64)
                    pe.matmul(psum[:, 4 + part_, 0:P], q2T[rows, hd, 0:P], k2T[rows, hd, 0:P], start=True, stop=True)
                    mm = pe.matmul(psum[:, 4 + part_, P:TRI], q2T[rows, hd, P:SEQ], k2T[rows, hd, :], start=True, stop=True)
                mm.then_inc(S["scores_done"], 1)

            def diff_turn(hd):
                pe.wait_ge(S["diff_a"], hd + 1)
                if hd >= 1:
                    pe.wait_ge(S["diff_aT"], hd)
                a = dff[:, hd % 2, :]
                pe.transpose(psum[:, 0, 0:P], a[:, 0:P], ident)
                pe.transpose(psum[:, 0, P:SEQ], a[:, P:SEQ], ident)
                pe.transpose(psum[:, 0, SEQ:TRI], a[:, SEQ:TRI], ident).then_inc(S["diff_turned"], 1)

            for g in range(2):
                pe.wait_ge(proj_used[g], 7)
            diff_scores(0)
            diff_scores(1)
            for hd in range(HEADS):
                diff_turn(hd)
                if hd + 2 < HEADS:
                    diff_scores(hd + 2)
                pe.wait_ge(S["diff_aT"], hd + 1)
                attend(2, hd, st[:, hd % 2, :], val2)
            project_out(1)
            route_and_experts(1)

        @block.scalar
        def _(act):
            turn = InTurn(act, S["act_turn"])

            def take_over_rounds(layer):
                with act.If(act.value_load(over_i[0:1, layer:layer + 1], min_val=0, max_val=SEQ) > SLOTS):
                    with act.Fori(0, OVER_ROUNDS) as r:
                        moe_act(act, layer, 1, r + 1)
                with act.Else():
                    act.nop()

            def keep_turned(dst, n):
                act.wait_ge(S["turned"], n)
                nc.scalar.copy(dst.rearrange("p (b a) t -> p b (a t)", b=2), psum[:, 6:8, :]).then_inc(S["turned_sb"], 1)

            def hT_half(n):
                act.wait_ge(S["h_turned"], n + 1)
                keep_hT(0, nc.scalar.copy).then_inc(S["hT_ready"], 1)

            def finish_mixer(layer):
                act.wait_ge(S["mix_turned"], layer + 1)
                keep_hT(0, nc.scalar.copy).then_inc(S["mixT_ready"], 1)
                act.wait_ge(S["added"], layer + 1)
                norm_act(act, turn, 2 * layer + 1)
                hT_half(2 * layer + 1)

            def route(layer):
                act.wait_ge(S["group_max"], layer + 1)
                nc.scalar.activation(rt[:, 0:8], rt[:, 0:8], ACT.Exp).then_inc(S["group_exp"], 1)
                act.wait_ge(S["top_diff"], layer + 1)
                nc.scalar.activation(rt[:, 8:10], rt[:, 8:10], ACT.Exp).then_inc(S["top_exp"], 1)

            act.wait_ge(S["x_landed"], 16)
            norm_act(act, turn, 0)
            act.wait_ge(S["rope_args"], 1)
            turn(nc.scalar.activation(cos_t, sin_t, ACT.Sin, scale=0.5))
            nc.scalar.activation(sin_t, sin_t, ACT.Sin).then_inc(S["rope_ready"], 1)
            hT_half(0)
            act.wait_ge(S["lb_in"], 1)
            nc.scalar.activation(lbt[:, :, :], lbt[:, :, :], ACT.Exp).then_inc(S["lb_exp"], 1)
            wait_projected(act, 1)
            nc.scalar.activation(tmp, flat(proj(0)), ACT.Exp, scale=-1.0)
            and_wait(act, nc.scalar.activation(flat(cumf), flat(proj(0)), ACT.Exp), S["f_exp"], 1)
            turn(nc.scalar.copy(small[0:1, 60:61], small[0:1, 0:1]))
            nc.scalar.copy(small[0:1, 61:62], small[0:1, 60:61]).then_inc(proj_used[0], 1)
            act.wait_ge(S["f_ready"], 1)
            nc.scalar.activation(tmp, tmp, ACT.Ln).then_inc(S["f_log"], 1)
            wait_projected(act, 2)
            nc.scalar.activation(flat(q2T), flat(proj(1)), ACT.Exp, scale=-1.0).then_inc(S["q_exp"], 1)
            act.wait_ge(S["mid_in"], 1)
            nc.scalar.activation(tmp, tmp, ACT.Exp).then_inc(S["mid_exp"], 1)

            def key_decays(hd):
                if hd == 0:
                    act.wait_ge(S["zeroed"], 1)
                else:
                    act.wait_ge(S["scores_done"], (0, 1, 2, 7)[hd])
                for dst, s0, i0 in ((ke0, 0, 0), (ke1, P, NSUB // 2)):
                    for i in range(i0, NSUB):
                        n = min(P, SUB * (i + 1) - s0)
                        ins = nc.scalar.activation(dst[:, i - i0, 0:n], cumf[:, hd, s0:s0 + n], ACT.Exp, scale=-1.0,
                                                   bias=cumf[:, hd, SUB * i + SUB // 2 - 1:SUB * i + SUB // 2])
                ins.then_inc(S["ke_exp"], 1)

            key_decays(0)
            wait_projected(act, 5)
            nc.scalar.copy(flat(val), flat(proj(4))).then_inc(S["val_ready"], 1)
            act.wait_ge(S["val_ready"], 1)
            nc.scalar.copy(small[0:1, 61:62], small[0:1, 60:61]).then_inc(proj_used[0], 1)
            keep_turned(qT, 1)
            keep_turned(kT, 2)
            key_decays(1)
            wait_projected(act, 6)
            nc.scalar.copy(flat(val2), flat(proj(5))).then_inc(S["val_ready"], 1)
            act.wait_ge(S["val_ready"], 2)
            nc.scalar.copy(small[0:1, 61:62], small[0:1, 60:61]).then_inc(proj_used[1], 1)
            key_decays(2)
            act.wait_ge(S["pv_done"], HEADS)
            nc.scalar.activation(tmp, flat(psum[:, 6:8, :]), ACT.Square).then_inc(S["sq_out"], 1)
            take_root(act, turn)
            key_decays(3)
            wait_projected(act, 7)
            act.wait_ge(S["out_used"], 1)
            nc.scalar.activation(tmp, flat(proj(6)), ACT.Exp, scale=-1.0).then_inc(S["gate_exp"], 1)
            wait_projected(act, 8)
            act.wait_ge(S["gated"], 1)
            nc.scalar.activation(tmp, flat(proj(7)), ACT.Exp, scale=-1.0).then_inc(S["gate_exp"], 1)
            act.wait_ge(S["pv_done"], 2 * HEADS)
            act.wait_ge(proj_used[1], 4)
            nc.scalar.activation(tmp, flat(psum[:, 6:8, :]), ACT.Square).then_inc(S["sq_out"], 1)
            take_root(act, turn)
            finish_mixer(0)
            route(0)
            moe_act(act, 0, 0, 0)
            take_over_rounds(0)

            act.wait_ge(S["finished_first"], 1)
            norm_act(act, turn, 2)
            hT_half(2)
            act.wait_ge(S["lam_dot"], 1)
            nc.scalar.activation(small[:, 40:42], small[:, 40:42], ACT.Exp).then_inc(S["lam_exp"], 1)
            for n in range(2):
                wait_projected(act, 9 + n)
                nc.scalar.copy((qT, kT)[n].rearrange("p h t -> p (h t)"), flat(proj(8 + n))).then_inc(S["turned_sb"], 1)
                act.wait_ge(S["turned_sb"], 3 + n)
                nc.scalar.copy(small[0:1, 61:62], small[0:1, 60:61]).then_inc(proj_used[n], 1)

            def stick_softplus(hd):
                act.wait_ge(S["stick_abs"], hd + 1)
                turn(nc.scalar.activation(sbe, sbe, ACT.Exp, scale=-1.0))
                nc.scalar.activation(sbe, sbe, ACT.Ln, bias=1.0).then_inc(S["stick_log"], 1)

            def stick_exp(hd):
                act.wait_ge(S["stick_arg"], hd + 1)
                nc.scalar.activation(sta[:, hd, :], sta[:, hd, :], ACT.Exp).then_inc(S["stick_a"], 1)

            for hd in range(HEADS):
                stick_softplus(hd)
                wait_projected(act, 11 + hd)
                if hd == 0:
                    nc.scalar.copy(flat(val), flat(proj(10))).then_inc(S["val_ready"], 1)
                    act.wait_ge(S["val_ready"], 3)
                    nc.scalar.copy(small[0:1, 61:62], small[0:1, 60:61]).then_inc(proj_used[0], 1)
                elif hd == 3:
                    nc.scalar.copy(flat(val2), flat(proj(13))).then_inc(S["val_ready"], 1)
                    act.wait_ge(S["val_ready"], 4)
                    nc.scalar.copy(small[0:1, 61:62], small[0:1, 60:61]).then_inc(proj_used[1], 1)
                else:
                    if hd == 2:
                        act.wait_ge(S["roped"], 3)
                    nc.scalar.activation(tmp1, flat(proj(10 + hd)), ACT.Square).then_inc(S["norm_sq"], 1)
                    take_root(act, turn)
                stick_exp(hd)
            keep_turned(q2T, 3)
            keep_turned(k2T, 4)

            def diff_exp(hd):
                act.wait_ge(S["diff_max"], hd + 1)
                s = dss[:, hd % 2]
                at = 16 * (hd % 2)
                for tc, cols in enumerate((slice(0, P), slice(P, TRI))):
                    for c in range(2):
                        j = at + 2 * tc + c
                        ins = nc.scalar.activation(s[:, c, cols], s[:, c, cols], ACT.Exp, bias=small[:, 8 + j:9 + j],
                                                   accum_out=small[:, 12 + j:13 + j])
                ins.then_inc(S["diff_exp"], 1)

            def diff_keep(hd):
                act.wait_ge(S["diff_turned"], hd + 1)
                nc.scalar.copy(st[:, hd % 2, :], psum[:, 0, 0:TRI]).then_inc(S["diff_aT"], 1)

            diff_exp(0)
            diff_exp(1)
            for hd in range(HEADS):
                if hd >= 2:
                    act.wait_ge(S["pv_done"], 3 * HEADS + hd - 1)
                diff_keep(hd)
                if hd + 2 < HEADS:
                    diff_exp(hd + 2)
            act.wait_ge(S["pv_done"], 4 * HEADS)
            nc.scalar.activation(tmp1, flat(psum[:, 2:4, :]), ACT.Square).then_inc(S["sq_out"], 1)
            take_root(act, turn)
            finish_mixer(1)
            route(1)
            moe_act(act, 1, 0, 0)
            take_over_rounds(1)

        @block.gpsimd
        def _(pool):
            pool.wait_ge(S["h_turned"], 1)
            nc.gpsimd.memset(ke0, 0.0)
            nc.gpsimd.memset(ke1, 0.0).then_inc(S["zeroed"], 1)

        @block.vector
        def _(dve):
            turn = InTurn(dve, S["dve_turn"])
            V = nc.vector

            def hT_half(n):
                dve.wait_ge(S["h_turned"], n + 1)
                keep_hT(1, V.tensor_copy).then_inc(S["hT_ready"], 1)

            def inverse_of_one_plus(a):
                turn(V.tensor_scalar(a, a, 1.0, None, ALU.add))
                turn(V.reciprocal(a, a))

            def finish_mixer(layer):
                dve.wait_ge(S["mix_turned"], layer + 1)
                keep_hT(1, V.tensor_copy).then_inc(S["mixT_ready"], 1)
                dve.wait_ge(S["unit_used"], moe_base(layer))
                for tc in range(TC):
                    r = V.tensor_tensor(x[:, tc, :], x[:, tc, :], flat(psum[:, 4 + 2 * tc:6 + 2 * tc, :]), ALU.add)
                and_wait(dve, r, S["added"], layer + 1)
                norm_dve(dve, turn, 2 * layer + 1)
                hT_half(2 * layer + 1)

            def rope_by_head(src, dst, width, cols, t1, t2):
                half = width // 2
                n = GROUP_W // width
                x1, x2 = src[:, :, :, 0:half], src[:, :, :, half:width]
                for_all = lambda tab: tab[:, :, cols].unsqueeze(2).broadcast_to([P, TC, n, half])
                c, s = for_all(cos_t), for_all(sin_t)
                turn(V.tensor_tensor(t1, x1, c, ALU.mult))
                turn(V.tensor_tensor(t2, x2, s, ALU.mult))
                turn(V.tensor_tensor(dst[:, :, :, 0:half], t1, t2, ALU.subtract))
                turn(V.tensor_tensor(t1, x2, c, ALU.mult))
                turn(V.tensor_tensor(t2, x1, s, ALU.mult))
                return V.tensor_tensor(dst[:, :, :, half:width], t1, t2, ALU.add)

            def inverse_rms(squares, col, count, width):
                r = small[:, col:col + count]
                turn(V.tensor_reduce(r, squares, AX, ALU.add))
                inverse_root(dve, V.tensor_scalar(r, r, 1.0 / width, EPS, ALU.mult, ALU.add), turn, col, count)
                return r

            def route(layer):
                def r3(at, n):
                    return rt[:, at:at + TC * n].rearrange("p (c n) -> p c n", c=TC)

                def over(a, n):
                    return a.unsqueeze(2).broadcast_to([P, TC, n])
                logits, gm, gs = r3(64, 36), rt[:, 10:12], rt[:, 12:14]
                g_hot, e_in, s32, hot1, hot2 = r3(160, 4), r3(192, 32), r3(256, 32), r3(320, 32), r3(384, 32)
                m1, m2, sc, pg = rt[:, 14:16], rt[:, 16:18], rt[:, 18:20], rt[:, 20:22]
                w1, w2 = rt[:, 22:24], rt[:, 24:26]
                gl = r3(0, 4)
                dve.wait_ge(S["logits_done"], layer + 1)
                bias = rb[:, layer, :].unsqueeze(1).broadcast_to([P, TC, 36])
                turn(V.tensor_tensor(logits, psum[:, 4, 0:72].rearrange("p (c n) -> p c n", c=TC), bias, ALU.add))
                turn(V.tensor_reduce(gm, logits[:, :, 0:4], AX, ALU.max))
                and_wait(dve, V.tensor_tensor(gl, logits[:, :, 0:4], over(gm, 4), ALU.subtract), S["group_max"], layer + 1)
                falling = const("falling").unsqueeze(1).broadcast_to([P, TC, 32])

                def first_hot(hot, values, top, n):
                    turn(V.tensor_tensor(hot, values, over(top, n), ALU.is_equal))
                    turn(V.tensor_tensor(hot, hot, falling[:, :, 0:n], ALU.mult))
                    turn(V.tensor_reduce(sc, hot, AX, ALU.max))
                    turn(V.tensor_tensor(hot, hot, over(sc, n), ALU.is_equal))
                first_hot(g_hot, logits[:, :, 0:4], gm, 4)
                turn(V.tensor_scalar(g_hot, g_hot, -1.0, BIG, ALU.add, ALU.mult))
                by_group = e_in.rearrange("p c (g e) -> p c g e", g=N_GROUPS)
                for tc in range(TC):
                    turn(V.tensor_tensor(by_group[:, tc], logits[:, tc, 4:36].rearrange("p (g e) -> p g e", g=N_GROUPS),
                                         g_hot[:, tc, :].unsqueeze(2).broadcast_to([P, N_GROUPS, PER_GROUP]), ALU.add))
                turn(V.tensor_reduce(m1, e_in, AX, ALU.max))
                first_hot(hot1, e_in, m1, 32)
                turn(V.tensor_scalar(s32, hot1, -BIG, None, ALU.mult))
                turn(V.tensor_tensor(s32, s32, e_in, ALU.add))
                turn(V.tensor_reduce(m2, s32, AX, ALU.max))
                first_hot(hot2, s32, m2, 32)
                and_wait(dve, V.tensor_tensor(rt[:, 8:10], m2, m1, ALU.subtract), S["top_diff"], layer + 1)
                and_wait(dve, V.tensor_tensor(picked, hot1, hot2, ALU.add), S["picked_ready"], layer + 1)
                dve.wait_ge(S["group_exp"], layer + 1)
                turn(V.tensor_reduce(gs, gl, AX, ALU.add))
                turn(V.reciprocal(pg, gs))
                dve.wait_ge(S["top_exp"], layer + 1)
                turn(V.tensor_scalar(w1, rt[:, 8:10], 1.0, None, ALU.add))
                turn(V.reciprocal(w1, w1))
                turn(V.tensor_tensor(w1, w1, pg, ALU.mult))
                turn(V.tensor_tensor(w2, w1, rt[:, 8:10], ALU.mult))
                turn(V.tensor_tensor(hot1, hot1, over(w1, 32), ALU.mult))
                turn(V.tensor_tensor(hot2, hot2, over(w2, 32), ALU.mult))
                turn(V.memset(rt[:, 0:4], 0.0))
                turn(V.memset(wtab.rearrange("p c e -> p (c e)"), 0.0))
                turn(V.memset(rank.rearrange("p c e -> p (c e)"), -1.0))
                turn(V.tensor_tensor(wtab[:, :, 0:32], hot1, hot2, ALU.add))
                dve.wait_ge(S["ranks_done"], layer + 1)
                turn(V.tensor_scalar(s32, psum[:, 5, 0:64].rearrange("p (c n) -> p c n", c=TC), 1.0, None, ALU.add))
                turn(V.tensor_tensor(s32, s32, picked, ALU.mult))
                turn(V.tensor_scalar(rank[:, :, 0:32], s32, -1.0, None, ALU.add))
                turn(V.tensor_reduce(sc[:, 0:1], psum[:, 5, 64:96], AX, ALU.max))
                and_wait(dve, V.tensor_copy(over_i[:, layer:layer + 1], sc[:, 0:1]), S["route_ready"], layer + 1)

            def take_over_rounds(layer):
                with dve.If(dve.value_load(over_i[0:1, layer:layer + 1], min_val=0, max_val=SEQ) > SLOTS):
                    with dve.Fori(0, OVER_ROUNDS) as r:
                        m = M[layer]
                        V.tensor_scalar(rank[:, :, :], rank[:, :, :], -float(SLOTS), None, ALU.add).then_inc(m["round_done"], 1)
                        dve.wait_ge(m["round_done"], r + 1)
                        moe_dve(dve, layer, 1, r + 1)
                with dve.Else():
                    dve.nop()

            dve.wait_ge(S["x_landed"], 16)
            norm_dve(dve, turn, 0)
            dve.wait_ge(S["small_landed"], 16 * N_SMALL)
            turn(V.tensor_copy(small[:, 5:7], pos_i[:, :]))
            for tc in range(TC):
                turn(V.tensor_scalar(sin_t[:, tc, :], const("inv_freq"), small[:, 5 + tc:6 + tc], None, ALU.mult))
            turn(V.tensor_scalar(cos_t, sin_t, 1 / (2 * math.pi), ROUND, ALU.mult, ALU.add))
            turn(V.tensor_scalar(cos_t, cos_t, -ROUND, None, ALU.add))
            turn(V.scalar_tensor_tensor(sin_t, cos_t, -TWO_PI_HI, sin_t, ALU.mult, ALU.add))
            turn(V.scalar_tensor_tensor(sin_t, cos_t, -TWO_PI_LO, sin_t, ALU.mult, ALU.add))
            and_wait(dve, V.tensor_scalar(sin_t, sin_t, 3.14159, -3.14159, ALU.min, ALU.max), S["rope_args"], 1)
            hT_half(0)
            lb4 = small[:, 44:48]
            turn(V.tensor_tensor(lb4, lbt[:, 0, :], lbt[:, 1, :], ALU.max))
            turn(V.tensor_tensor(lb4, lb4, lbt[:, 2, :], ALU.max))
            and_wait(dve, V.tensor_tensor(lbt[:, :, :], lbt[:, :, :], lb4.unsqueeze(1).broadcast_to([P, 3, HEADS]), ALU.subtract),
                     S["lb_in"], 1)
            dve.wait_ge(S["lb_exp"], 1)
            turn(V.tensor_tensor(lb4, lbt[:, 0, :], lbt[:, 1, :], ALU.add))
            turn(V.tensor_tensor(lb4, lb4, lbt[:, 2, :], ALU.add))
            turn(V.reciprocal(lb4, lb4))
            turn(V.tensor_tensor(lbw[:, 0, :], lbt[:, 0, :], lb4, ALU.mult))
            turn(V.tensor_scalar(lbw[:, 1, :], lbw[:, 0, :], -1.0, 1.0, ALU.mult, ALU.add))
            dve.wait_ge(S["rope_ready"], 1)
            turn(V.tensor_tensor(cos_t, cos_t, cos_t, ALU.mult))
            turn(V.tensor_scalar(cos_t, cos_t, -2.0, 1.0, ALU.mult, ALU.add))
            dve.wait_ge(S["f_exp"], 1)
            inverse_of_one_plus(tmp)
            inverse_of_one_plus(flat(cumf))
            for hd in range(HEADS):
                cols = slice(hd * SEQ, (hd + 1) * SEQ)
                turn(V.tensor_scalar(k2T[:, hd, :], cumf[:, hd, :], lbw[:, 1, hd:hd + 1], None, ALU.mult))
                turn(V.tensor_scalar(tmp[:, cols], tmp[:, cols], lbw[:, 1, hd:hd + 1], lbw[:, 0, hd:hd + 1], ALU.mult, ALU.add))
            and_wait(dve, V.tensor_scalar(tmp, tmp, F_FLOOR, None, ALU.max), S["f_ready"], 1)
            dve.wait_ge(S["f_log"], 1)
            for hd in range(HEADS):
                r = V.tensor_tensor_scan(cumf[:, hd, :], ones, tmp[:, hd * SEQ:(hd + 1) * SEQ], 0.0, ALU.mult, ALU.add)
            and_wait(dve, r, S["cum_ready"], 1)
            sub = flat(cumf).rearrange("p (i s) -> p i s", s=SUB)
            and_wait(dve, V.tensor_tensor(tmp.rearrange("p (i s) -> p i s", s=SUB), sub,
                                          sub[:, :, SUB // 2 - 1].unsqueeze(2).broadcast_to([P, HEADS * NSUB, SUB]), ALU.subtract),
                     S["mid_in"], 1)
            dve.wait_ge(S["q_exp"], 1)
            inverse_of_one_plus(flat(q2T))
            and_wait(dve, V.tensor_tensor(flat(q2T), flat(proj(1)), flat(q2T), ALU.mult), proj_used[1], 1)
            dve.wait_ge(S["mid_exp"], 1)
            and_wait(dve, V.tensor_tensor(flat(q2T), flat(q2T), tmp, ALU.mult), S["qe_ready"], 1)

            def rope_ret(g, col):
                wait_projected(dve, g + 1)
                t12 = tmp.rearrange("p (a c h d) -> p a c h d", a=2, c=TC, h=HEADS)
                and_wait(dve, rope_by_head(heads(proj(g)), heads(mixed[:, :, col:col + GROUP_W]), HD, slice(0, 64),
                                           t12[:, 0], t12[:, 1]), S["roped"], g - 1)
                V.memset(small[:, 4:5], 0.0).then_inc(proj_used[g % 2], 1)

            def key_products(hd):
                dve.wait_ge(S["ke_exp"], hd + 1)
                for part_, s0, i0 in ((ke0, 0, 0), (ke1, P, NSUB // 2)):
                    V.tensor_tensor(part_, part_, k2T[:, hd, s0:s0 + P].unsqueeze(1).broadcast_to([P, NSUB - i0, P]),
                                    ALU.mult).then_inc(S["ke_ready"], 1)

            def mask(k, bank, dst, table):
                dve.wait_ge(S["scores_done"], k + 1)
                V.tensor_tensor(dst, psum[:, bank, 0:TRI], table, ALU.mult).then_inc(S["st_ready"], 1)

            def silu_gate(g, dst):
                dve.wait_ge(S["gate_exp"], g - 5)
                inverse_of_one_plus(tmp)
                and_wait(dve, V.tensor_tensor(dst, flat(proj(g)), tmp, ALU.mult), proj_used[g % 2], 4)

            def gated_norm(which, gate, col):
                dve.wait_ge(S["sq_out"], which + 1)
                r = inverse_rms(tmp.rearrange("p (n d) -> p n d", d=HD), 20 + 8 * which, 8, HD)
                out = mixed[:, :, col:col + GROUP_W]
                o = heads(psum[:, 6:8, :])
                and_wait(dve, V.tensor_tensor(heads(out), o, r.rearrange("p (c h) -> p c h", c=TC).unsqueeze(3)
                                              .broadcast_to([P, TC, HEADS, HD]), ALU.mult), S["out_used"], which + 1)
                g = retg[:, which, :].unsqueeze(1).broadcast_to([P, TC, GROUP_W])
                turn(V.tensor_tensor(out, out, g, ALU.mult))

            def gate_it(which, gate, col):
                out = mixed[:, :, col:col + GROUP_W]
                V.tensor_tensor(out, out, gate.rearrange("p h t -> p (h t)").rearrange("p (c n) -> p c n", c=TC),
                                ALU.mult).then_inc(S["gated"], 1)

            decay = lambda hd: const("decay")[:, hd * TRI:(hd + 1) * TRI]
            rope_ret(2, 0)
            rope_ret(3, GROUP_W)
            key_products(0)
            mask(0, 4, st2[:, 0, :], const("causal_scale"))
            key_products(1)
            mask(1, 5, st2[:, 1, :], const("causal_scale"))
            for hd in range(HEADS):
                if hd >= 2:
                    dve.wait_ge(S["pv_done"], hd - 1)
                mask(2 + hd, 4 + hd % 2, st[:, hd % 2, :], decay(hd))
            key_products(2)
            gated_norm(0, None, 0)
            mask(6, 4, st2[:, 2, :], const("causal_scale"))
            key_products(3)
            silu_gate(6, flat(kT))
            gate_it(0, kT, 0)
            mask(7, 5, st2[:, 3, :], const("causal_scale"))
            silu_gate(7, flat(qT))
            gated_norm(1, None, GROUP_W)
            gate_it(1, qT, GROUP_W)
            finish_mixer(0)
            route(0)
            moe_dve(dve, 0, 0, 0)
            take_over_rounds(0)
            turn(V.memset(small[:, 4:5], 0.0))
            V.memset(small[:, 4:5], 0.0).then_inc(S["finished_first"], 1)

            norm_dve(dve, turn, 2)
            hT_half(2)
            for i in range(2):
                turn(V.tensor_tensor(dlam[:, 2 * i, :], dlam[:, 2 * i, :], dlam[:, 2 * i + 1, :], ALU.mult))
                r = V.tensor_reduce(small[:, 40 + i:41 + i], dlam[:, 2 * i, :], AX, ALU.add)
            and_wait(dve, r, S["lam_dot"], 1)
            dve.wait_ge(S["lam_exp"], 1)
            neg_lam = small[:, 42:43]
            turn(V.tensor_tensor(neg_lam, small[:, 41:42], small[:, 40:41], ALU.subtract))
            turn(V.tensor_scalar(neg_lam, neg_lam, -LAM_INIT, None, ALU.add))

            def stick_in(hd):
                dve.wait_ge(S["scores_done"], 8 + hd + 1)
                turn(V.tensor_scalar(sbz[:, 0, :], psum[:, 4, 0:TRI], SCALE, None, ALU.mult))
                and_wait(dve, V.scalar_tensor_tensor(sbe, sbz[:, 0, :], -1.0, sbz[:, 0, :], ALU.mult, ALU.max), S["stick_abs"], hd + 1)

            def stick_l(hd):
                dve.wait_ge(S["stick_log"], hd + 1)
                turn(V.scalar_tensor_tensor(sbl, sbz[:, 0, :], 0.0, sbe, ALU.max, ALU.add))
                and_wait(dve, V.tensor_tensor(sbl, sbl, const("strict"), ALU.mult), S["stick_l"], hd + 1)
                turn(V.tensor_tensor(sbz[:, 1, :], sbz[:, 0, :], const("strict_add"), ALU.add))

            def stick_out(hd):
                dve.wait_ge(S["stick_r"], hd + 1)
                and_wait(dve, V.tensor_tensor(sta[:, hd, :], sbz[:, 1, :], psum[:, 5, 0:TRI], ALU.subtract),
                         S["stick_arg"], hd + 1)

            def qk_norm_rope(n):
                g = 11 + n
                dve.wait_ge(S["norm_sq"], n + 1)
                r = inverse_rms(tmp1.rearrange("p (n d) -> p n d", d=64), 44, 16, 64)
                by = lambda a: a.rearrange("p c (h d) -> p c h d", d=64)
                y = tmp1.rearrange("p (c n d) -> p c n d", c=TC, d=64)
                and_wait(dve, V.tensor_tensor(y, by(proj(g)), r.rearrange("p (c n) -> p c n", c=TC).unsqueeze(3)
                                              .broadcast_to([P, TC, 8, 64]), ALU.mult), proj_used[g % 2], 6 + n)
                turn(V.tensor_tensor(tmp1.rearrange("p (n d) -> p n d", d=64), tmp1.rearrange("p (n d) -> p n d", d=64),
                                     dg[:, n, :].unsqueeze(1).broadcast_to([P, 16, 64]), ALU.mult))
                t12 = tmp2.rearrange("p (a c h d) -> p a c h d", a=2, c=TC, d=32)
                and_wait(dve, rope_by_head(y, by(mixed[:, :, n * GROUP_W:(n + 1) * GROUP_W]), 64, slice(64, 96),
                                           t12[:, 0], t12[:, 1]), S["roped"], 3 + n)

            stick_in(0)
            for hd in range(HEADS):
                stick_l(hd)
                stick_out(hd)
                if hd + 1 < HEADS:
                    stick_in(hd + 1)
                if hd in (1, 2):
                    qk_norm_rope(hd - 1)

            def diff_in(hd):
                dve.wait_ge(S["scores_done"], 12 + hd + 1)
                s = dss[:, hd % 2]
                for c in range(2):
                    r = V.scalar_tensor_tensor(s[:, c, :], psum[:, 4 + c, 0:TRI], SCALE_DIFF, const("causal_add"),
                                               ALU.mult, ALU.add)
                and_wait(dve, r, S["diff_in"], hd + 1)
                at = 8 + 16 * (hd % 2)
                turn(V.tensor_reduce(small[:, at:at + 2], s[:, :, 0:P], AX, ALU.max))
                turn(V.tensor_reduce(small[:, at + 2:at + 4], s[:, :, P:TRI], AX, ALU.max))
                V.tensor_scalar(small[:, at:at + 4], small[:, at:at + 4], -1.0, None, ALU.mult).then_inc(S["diff_max"], 1)

            def diff_out(hd):
                dve.wait_ge(S["diff_exp"], hd + 1)
                if hd >= 2:
                    dve.wait_ge(S["diff_turned"], hd - 1)
                s, a = dss[:, hd % 2], dff[:, hd % 2, :]
                at = 12 + 16 * (hd % 2)
                turn(V.reciprocal(small[:, at:at + 4], small[:, at:at + 4]))
                for tc in range(TC):
                    k = small[:, at + 2 * tc + 1:at + 2 * tc + 2]
                    turn(V.tensor_tensor(k, k, neg_lam, ALU.mult))
                for tc, cols in enumerate((slice(0, P), slice(P, TRI))):
                    turn(V.tensor_scalar(a[:, cols], s[:, 0, cols], small[:, at + 2 * tc:at + 2 * tc + 1], None, ALU.mult))
                    r = V.scalar_tensor_tensor(a[:, cols], s[:, 1, cols], small[:, at + 2 * tc + 1:at + 2 * tc + 2],
                                               a[:, cols], ALU.mult, ALU.add)
                and_wait(dve, r, S["diff_a"], hd + 1)

            diff_in(0)
            dve.wait_ge(S["pv_done"], 3 * HEADS)
            V.tensor_copy(mixed[:, :, 0:GROUP_W], psum[:, 6:8, :]).then_inc(S["gated"], 1)
            diff_in(1)
            for hd in range(HEADS):
                diff_out(hd)
                if hd + 2 < HEADS:
                    diff_in(hd + 2)
            dve.wait_ge(S["sq_out"], 3)
            r = inverse_rms(tmp1.rearrange("p (n d) -> p n d", d=HD), 44, 8, HD)
            out = mixed[:, :, GROUP_W:D]
            turn(V.tensor_scalar(r, r, 1.0 - LAM_INIT, None, ALU.mult))
            turn(V.tensor_tensor(heads(out), heads(psum[:, 2:4, :]), r.rearrange("p (c h) -> p c h", c=TC).unsqueeze(3)
                                 .broadcast_to([P, TC, HEADS, HD]), ALU.mult))
            for tc in range(TC):
                r = V.tensor_tensor(mixed[:, tc, GROUP_W:D].rearrange("p (h d) -> p h d", d=HD),
                                    mixed[:, tc, GROUP_W:D].rearrange("p (h d) -> p h d", d=HD),
                                    subln[:, :].unsqueeze(1).broadcast_to([P, HEADS, HD]), ALU.mult)
            r.then_inc(S["gated"], 1)
            finish_mixer(1)
            route(1)
            moe_dve(dve, 1, 0, 0)
            take_over_rounds(1)
            turn(V.memset(small[:, 4:5], 0.0))
            V.memset(small[:, 4:5], 0.0).then_inc(S["finished"], 1)


PARAMS = ["x", "positions", "norm_mix", "norm_ffn", "w_in_ab", "w_out_ab", "ret_gnorm", "hgrn_lb_logits",
          "hgrn_onorm", "w_in_cd", "w_out_cd", "diff_qnorm", "diff_knorm", "diff_lam_q1", "diff_lam_k1",
          "diff_lam_q2", "diff_lam_k2", "diff_subln", "router_group_w", "router_group_b",
          "router_expert_w", "router_expert_b", "w_gate", "w_up", "w_down"]


def kernel(**inputs):
    import concourse.bacc as bacc
    from concourse.bass_utils import run_bass_kernel_spmd

    nc = bacc.Bacc("TRN2", target_bir_lowering=False, num_devices=1)
    consts, where = shape_constants()
    arrays = {f"in_{n}": np.ascontiguousarray(inputs[n]) for n in PARAMS}
    arrays["in_consts"] = consts
    t = {n[3:]: nc.dram_tensor(n, a.shape, mybir.dt.from_np(a.dtype), kind="ExternalInput").ap()
         for n, a in arrays.items()}
    t["out"] = nc.dram_tensor("out", (1, SEQ, D), F32, kind="ExternalOutput").ap()
    build(nc, t, where, consts.shape[1])
    r = run_bass_kernel_spmd(nc, [arrays], core_ids=[0])
    return r.results[0]["out"]
```

```python
from contextlib import ExitStack
import math

import numpy as np
import concourse.bass as bass
from concourse import mybir

ALU = mybir.AluOpType
ACT = mybir.ActivationFunctionType
F32 = mybir.dt.float32
I32 = mybir.dt.int32
AX = mybir.AxisListType.X

P = 128
SEQ = 256
D = 1024
LOG_EXP = "natural_log_exp_and_others"
TC = SEQ // P
KC = D // P
HEADS = 4
HD = 128
GROUP_W = HEADS * HD
EPS = 1e-6
SUB = 16
NSUB = SEQ // SUB
N_GROUPS = 4
PER_GROUP = 8
N_EXPERTS = N_GROUPS * PER_GROUP
FF = 512
FC = FF // P
SLOTS = 64
PAIRS = N_EXPERTS // 2
OVER_ROUNDS = SEQ // SLOTS - 1
FIRST_CONSTS = P + 96
N_SMALL = 20
RING = 6
UNIT = 4096
UNITS_IN = (8, 6)
UNITS_OUT = 2
UNITS_PAIR = 6
BIG = 1e30
LAM_INIT = 0.8 - 0.6 * math.exp(-0.3 * 1)
TWO_PI_HI = 6.28125
TWO_PI_LO = 2 * math.pi - 6.28125
ROUND = 1.5 * 2.0 ** 23
F_FLOOR = math.exp(-10.0)
K_FLOOR = 1e-18
SCALE = HD ** -0.5
SCALE_DIFF = 64 ** -0.5
TRI = 384

BLOCKS = ((5, 4, 0, 1, 2, 6, 3, 7), (0, 1, 3, 4, 5, 2))
TURNED = ((5, 4), (0, 1))

ROOTS = ((2, 2), (20, 8), (28, 8), (2, 2), (2, 2), (44, 16), (44, 16), (44, 8), (2, 2))


def shape_constants():
    p = np.arange(P)[:, None]
    f128, f256 = np.arange(P)[None, :], np.arange(SEQ)[None, :]
    parts = {}
    inv = [1.0 / (np.float32(10000.0) ** (np.arange(0, d, 2, dtype=np.float32) / np.float32(d))) for d in (128, 64)]
    parts["ident"] = (p == f128)
    parts["inv_freq"] = np.broadcast_to(np.concatenate(inv)[None, :], (P, 96))
    parts["before"] = (p < f128)
    parts["from_on"] = (p >= f128)
    parts["ones"] = np.ones((P, SEQ))
    parts["iota"] = np.broadcast_to(np.arange(SLOTS)[None, :], (P, SLOTS))
    parts["falling"] = np.broadcast_to((N_EXPERTS - np.arange(N_EXPERTS))[None, :], (P, N_EXPERTS))
    le = np.concatenate([p <= f256, p <= f128], 1)
    lt = np.concatenate([p < f256, p < f128], 1)
    rel = np.concatenate([f256 - p, f128 - p], 1).astype(np.float64)
    parts["decay"] = np.concatenate(
        [np.where(rel >= 0, (1 - 2.0 ** (-5 - h)) ** np.maximum(rel, 0), 0.0) * SCALE for h in range(HEADS)], 1)
    parts["causal_scale"] = le * SCALE
    parts["strict"] = lt
    parts["strict_add"] = np.where(lt, 0.0, -BIG)
    low = p >= f128
    parts["causal_add"] = np.where(np.concatenate([low, np.ones((P, P), bool), low], 1), 0.0, -BIG)
    where, at = {}, 0
    for name, a in parts.items():
        where[name] = (at, at + a.shape[1])
        at += a.shape[1]
    return np.ascontiguousarray(np.concatenate([a.astype(np.float32) for a in parts.values()], 1)), where


class InTurn:

    def __init__(self, eng, sem, base=0):
        self.eng, self.sem, self.base, self.n = eng, sem, base, 0

    def __call__(self, instruction):
        self.n += 1
        instruction.then_inc(self.sem, 1)
        self.eng.wait_ge(self.sem, self.base + self.n)


def build(nc, t, where, const_width, stop_after=4):
    with ExitStack() as ctx:
        def sb(name, shape, dt=F32):
            return ctx.enter_context(nc.sbuf_tensor(name, shape, dt))

        def sem(name):
            return ctx.enter_context(nc.semaphore(name))

        ring = sb("ring", [P, RING, UNIT])
        consts = sb("consts", [P, const_width])
        x = sb("x", [P, TC, D])
        h = sb("h", [P, TC, KC, P])
        hT = sb("hT", [P, KC, SEQ])
        mixed = sb("mixed", [P, TC, D])
        gain = sb("gain", [P, D])
        small = sb("small", [P, 96])
        pos_i = sb("pos_i", [P, TC], I32)
        rope = sb("rope", [P, 2, TC, 96])
        psum = ctx.enter_context(nc.psum_tensor("psum", [P, 8, 512], F32))

        def const(name):
            return consts[:, where[name][0]:where[name][1]]

        ident, before, from_on = const("ident"), const("before"), const("from_on")
        ones = const("ones")
        sin_t, cos_t = rope[:, 0], rope[:, 1]

        arena_w = 12416
        arena = sb("arena", [P, arena_w])
        taken = {}

        def part(who, width, shape=None, **dims):
            a = taken.get(who, 0)
            taken[who] = a + width
            assert taken[who] <= arena_w, (who, taken)
            v = arena[:, a:a + width]
            return v.rearrange(shape, **dims) if shape else v

        qT = part("mix", 1024, "p (h t) -> p h t", h=HEADS)
        kT = part("mix", 1024, "p (h t) -> p h t", h=HEADS)
        q2T = part("mix", 1024, "p (h t) -> p h t", h=HEADS)
        k2T = part("mix", 1024, "p (h t) -> p h t", h=HEADS)
        val = part("mix", 1024, "p (c n) -> p c n", c=TC)
        val2 = part("mix", 1024, "p (c n) -> p c n", c=TC)
        st = part("mix", 2 * TRI, "p (b n) -> p b n", b=2)
        keep_mix = taken["mix"]
        cumf = part("mix", 1024, "p (h t) -> p h t", h=HEADS)
        tmp = part("mix", 1024)
        st2 = part("mix", HEADS * TRI, "p (h n) -> p h n", h=HEADS)
        ke0 = h[:, :, :, :].rearrange("p a b s -> p (a b) s")
        ke1 = part("mix", NSUB // 2 * P, "p (i s) -> p i s", s=P)
        taken["mix1"] = keep_mix
        h_flat = h[:, :, :, :].rearrange("p a b s -> p (a b s)")
        sta = h_flat[:, 0:HEADS * TRI].rearrange("p (h n) -> p h n", h=HEADS)
        sbe = h_flat[:, HEADS * TRI:(HEADS + 1) * TRI]
        sbz = part("mix1", 2 * TRI, "p (b n) -> p b n", b=2)
        sbl = part("mix1", TRI)
        dss = part("mix1", 4 * TRI, "p (b c n) -> p b c n", b=2, c=2)
        dff = part("mix1", 2 * TRI, "p (b n) -> p b n", b=2)
        tmp1 = part("mix1", 1024)
        tmp2 = part("mix1", 1024)
        xT = part("moe", KC * P, "p (c s) -> p c s", c=KC)
        sel = part("moe", TC * P, "p (c s) -> p c s", c=TC)
        selw = part("moe", TC * P, "p (c s) -> p c s", c=TC)
        spread = part("moe", TC * P, "p (c t) -> p c t", c=TC)
        sig = part("moe", FF)
        act_h = part("moe", FF, "p (c s) -> p c s", c=FC)
        actT = part("moe", FC * P, "p (c s) -> p c s", c=FC)
        y_sb = part("moe", D)
        rt = part("moe", 2048)
        rank = part("moe", TC * (N_EXPERTS + 2), "p (c e) -> p c e", c=TC)
        wtab = part("moe", TC * (N_EXPERTS + 2), "p (c e) -> p c e", c=TC)
        picked = part("moe", TC * N_EXPERTS, "p (c e) -> p c e", c=TC)
        rw = sb("rw", [P, 2, KC, 36])
        rb = sb("rb", [P, 2, 36])
        gcol = sb("gcol", [P, 2, KC])
        lbt = sb("lbt", [P, 3, HEADS])
        lbw = sb("lbw", [P, 4, HEADS])
        retg = sb("retg", [P, 2, GROUP_W])
        dg = sb("dg", [P, 2, 64])
        dlam = sb("dlam", [P, 4, 64])
        subln = sb("subln", [P, HD])
        over_i = sb("over_i", [P, 2], I32)

        names = ["small_landed", "x_landed", "first_landed", "pos_landed", "lb_landed", "gain_landed", "gain_used", "unit_used", "stored",
                 "act_turn", "dve_turn", "rope_args", "rope_ready", "zeroed", "pos_ready",
                 "squares", "normed", "h_turned", "hT_ready", "lb_in", "lb_exp",
                 "f_sig", "keys_log", "f_ready", "f_log", "cum_ready", "q_sig", "mid_in", "mid_exp", "qe_ready",
                 "ke_ready", "scores_done", "st_ready", "pv_done", "sq_out", "out_used",
                 "roped", "turned", "turned_sb", "val_ready", "gate_sig", "gated", "mix_turned", "mixT_ready",
                 "out_first", "added", "finished", "finished_first",
                 "stick_abs", "stick_log", "stick_l", "stick_r", "stick_arg", "stick_a",
                 "diff_in", "diff_max", "diff_exp", "diff_a", "diff_turned", "diff_aT", "lam_dot", "lam_exp",
                 "logits_done", "group_max", "group_exp", "top_diff", "top_exp", "picked_ready", "ranks_done",
                 "route_ready", "norm_sq", "root_in", "root_out", "router_ready"]
        S = {n: sem(n) for n in names}
        proj_used = [sem(f"proj_used{i}") for i in range(2)]
        landed = [sem(f"landed{i}") for i in range(RING)]
        over_landed = {(l, i): sem(f"over{l}_landed{i}") for l in range(2) for i in range(RING)}
        MOE_NAMES = ["sel_ready", "gathered", "xT_ready", "sig_ready", "act_ready",
                     "turned", "actT_ready", "y_ready", "spread_done", "round_done", "added",
                     "turn", "used"]
        M = {l: {n: sem(f"moe{l}_{n}") for n in MOE_NAMES} for l in range(2)}

        block = ctx.enter_context(nc.Block())

        def unit_base(layer):
            return layer * (UNITS_IN[0] + UNITS_OUT + UNITS_PAIR * PAIRS)

        def moe_base(layer):
            return unit_base(layer) + UNITS_IN[layer] + UNITS_OUT

        def wait_unit(eng, u):
            eng.wait_ge(landed[u % RING], 16 * (u // RING + 1))

        def and_wait(eng, instruction, signal, value):
            instruction.then_inc(signal, 1)
            eng.wait_ge(signal, value)

        def proj(g):
            return psum[:, 2 * (g % 2):2 * (g % 2) + 2, :]

        def wait_projected(eng, n):
            eng.wait_ge(S["unit_used"], n if n <= UNITS_IN[0] else unit_base(1) + n - UNITS_IN[0])

        def flat(a):
            return a.rearrange("p a b -> p (a b)")

        def heads(a):
            return a.rearrange("p c (h d) -> p c h d", h=HEADS)

        @block.sync
        def _(sp):
            w_in = (t["w_in_ab"], t["w_in_cd"])
            w_out = (t["w_out_ab"], t["w_out_cd"])

            def load_unit(u, dst_cols, src):
                if u >= RING:
                    sp.wait_ge(S["unit_used"], u - RING + 1)
                sp.dma_start(dst_cols(ring[:, u % RING, :]), src).then_inc(landed[u % RING], 16)

            def pair_units(layer, pair):
                for w, rows in (("w_gate", KC), ("w_up", KC), ("w_down", FC)):
                    for e in range(2):
                        yield t[w][layer, bass.ds(2 * pair + e, 1)].rearrange("a (p c) n -> p (a c n)", c=rows)

            sp.dma_start(x[:, :, :], t["x"].rearrange("b (c p) d -> p (b c) d", p=P)).then_inc(S["x_landed"], 16)
            sp.dma_start(consts[:, 0:FIRST_CONSTS], t["consts"][:, 0:FIRST_CONSTS]).then_inc(S["first_landed"], 16)
            sp.dma_start(gain[:, :], t["norm_mix"][0:1, :].broadcast_to([P, D])).then_inc(S["gain_landed"], 16)

            def load_in(layer, n):
                b = BLOCKS[layer][n]
                src = w_in[layer][0].rearrange("(p c) n -> p c n", c=KC)[:, :, b * 512:(b + 1) * 512]
                load_unit(unit_base(layer) + n, lambda s: s.rearrange("p (c n) -> p c n", c=KC), src)

            load_in(0, 0)
            with nc.allow_non_contiguous_dma("small tables"):
                sp.dma_start(pos_i[:, :], t["positions"].rearrange("b (c p) -> p (b c)", p=P)).then_inc(S["pos_landed"], 16)
                sp.dma_start(lbt[:, :, :], t["hgrn_lb_logits"].rearrange("r (h p) -> p r h", p=P)).then_inc(S["lb_landed"], 16)
                load_in(0, 1)
                small_loads = [
                    (consts[:, FIRST_CONSTS:], t["consts"][:, FIRST_CONSTS:]),
                    (retg[:, 0, :], t["ret_gnorm"].rearrange("a h d -> a (h d)").broadcast_to([P, GROUP_W])),
                    (retg[:, 1, :], t["hgrn_onorm"].rearrange("a h d -> a (h d)").broadcast_to([P, GROUP_W])),
                    (dg[:, 0, :], t["diff_qnorm"].broadcast_to([P, 64])),
                    (dg[:, 1, :], t["diff_knorm"].broadcast_to([P, 64])),
                    (dlam[:, 0, :], t["diff_lam_q1"].broadcast_to([P, 64])),
                    (dlam[:, 1, :], t["diff_lam_k1"].broadcast_to([P, 64])),
                    (dlam[:, 2, :], t["diff_lam_q2"].broadcast_to([P, 64])),
                    (dlam[:, 3, :], t["diff_lam_k2"].broadcast_to([P, 64])),
                    (subln[:, :], t["diff_subln"].broadcast_to([P, HD])),
                ]
                for l in range(2):
                    small_loads.append((gcol[:, l, :], t["norm_ffn"][l].rearrange("(c p) -> p c", p=P)))
                    small_loads.append((rw[:, l, :, 0:4], t["router_group_w"][l].rearrange("(c p) n -> p c n", p=P)))
                    small_loads.append((rw[:, l, :, 4:36], t["router_expert_w"][l].rearrange("(c p) n -> p c n", p=P)))
                    small_loads.append((rb[:, l, 0:4], t["router_group_b"][l:l + 1, :].broadcast_to([P, 4])))
                    small_loads.append((rb[:, l, 4:36], t["router_expert_b"][l:l + 1, :].broadcast_to([P, 32])))
                for dst, src in small_loads:
                    sp.dma_start(dst, src).then_inc(S["small_landed"], 16)
            assert len(small_loads) == N_SMALL

            for layer in range(2):
                base = unit_base(layer)
                for n in range(2 if layer == 0 else 0, UNITS_IN[layer]):
                    load_in(layer, n)
                sp.wait_ge(S["gain_used"], 2 * layer + 1)
                sp.dma_start(gain[:, :], t["norm_ffn"][layer:layer + 1, :].broadcast_to([P, D])).then_inc(S["gain_landed"], 16)
                for n in range(UNITS_OUT):
                    src = w_out[layer][0, 512 * n:512 * (n + 1), :].rearrange("(c p) n -> p c n", p=P)
                    load_unit(base + UNITS_IN[layer] + n, lambda s: s.rearrange("p (c n) -> p c n", c=4), src)
                mb = moe_base(layer)
                with sp.Fori(0, PAIRS) as i:
                    for j, src in enumerate(pair_units(layer, i)):
                        sp.wait_ge(S["unit_used"], i * UNITS_PAIR + (mb + 2 * (j // 2) + 2 - RING))
                        sp.dma_start(ring[:, (mb + j) % RING, :], src).then_inc(landed[(mb + j) % RING], 16)
                sp.wait_ge(S["route_ready"], layer + 1)
                count = sp.value_load(over_i[0:1, layer:layer + 1], min_val=0, max_val=SEQ)
                with sp.If(count > SLOTS):
                    sp.wait_ge(S["unit_used"], mb + UNITS_PAIR * PAIRS)
                    m = M[layer]
                    for j, src in enumerate(pair_units(layer, 0)):
                        sp.dma_start(ring[:, j, :], src).then_inc(over_landed[layer, j], 16)

                    def over_pair(n, pair):
                        for j, src in enumerate(pair_units(layer, pair)):
                            sp.wait_ge(m["used"], (n - 1) * UNITS_PAIR + (2 * (j // 2) + 2))
                            sp.dma_start(ring[:, j, :], src).then_inc(over_landed[layer, j], 16)

                    with sp.Fori(1, PAIRS) as i:
                        over_pair(i, i)
                    with sp.Fori(1, OVER_ROUNDS) as r:
                        with sp.Fori(0, PAIRS) as i:
                            over_pair(r * PAIRS + i, i)
                    sp.wait_ge(m["used"], OVER_ROUNDS * PAIRS * UNITS_PAIR)
                with sp.Else():
                    sp.nop()
                if layer == 0:
                    sp.wait_ge(S["gain_used"], 2)
                    sp.dma_start(gain[:, :], t["norm_mix"][1:2, :].broadcast_to([P, D])).then_inc(S["gain_landed"], 16)
            sp.wait_ge(S["finished"], 1)
            sp.dma_start(t["out"].rearrange("b (c p) d -> p (b c) d", p=P), x[:, :, :]).then_inc(S["stored"], 16)
            sp.wait_ge(S["stored"], 16)

        ACC, GATE, UP, YB = 0, 4, 5, 6

        def wait_pair(eng, layer, rnd, i, units):
            if isinstance(rnd, int):
                eng.wait_ge(S["unit_used"], i * UNITS_PAIR + (moe_base(layer) + units))
            else:
                eng.wait_ge(M[layer]["used"], (rnd - 1) * (PAIRS * UNITS_PAIR) + i * UNITS_PAIR + units)

        def moe_pe(pe, layer, over, rnd):
            m = M[layer]
            n17, n16 = rnd * (PAIRS + 1), rnd * PAIRS
            mb = moe_base(layer)

            def gather():
                for c in range(KC):
                    for tc in range(TC):
                        mm = pe.matmul(psum[:, YB + c // 4, (c % 4) * P:(c % 4 + 1) * P], h[:, tc, c, :],
                                       sel[:, tc, :], start=tc == 0, stop=tc == TC - 1)
                mm.then_inc(m["gathered"], 1)

            def spread_back():
                for tc in range(TC):
                    for n in range(2):
                        mm = pe.matmul(psum[:, ACC + 2 * tc + n, :], spread[:, tc, :],
                                       y_sb[:, 512 * n:512 * (n + 1)], start=False, stop=False,
                                       skip_group_check=True)
                mm.then_inc(m["spread_done"], 1)

            def unit(i, j):
                if over:
                    pe.wait_ge(over_landed[layer, j], ((rnd - 1) * PAIRS + i + 1) * 16)
                    return ring[:, j, :]
                u = mb + j
                pe.wait_ge(landed[u % RING], i * 16 + 16 * (u // RING + 1))
                return ring[:, u % RING, :]

            used = m["used"] if over else S["unit_used"]
            pe.wait_ge(m["y_ready"], 2 * (n17 + 1))
            for b in range(4):
                pe.matmul(psum[:, ACC + b, :], spread[:, 0, :], y_sb[:, 0:512], start=True, stop=False,
                          skip_group_check=True)
            pe.wait_ge(m["sel_ready"], n17 + 1)
            pe.wait_ge(S["normed"], TC * (2 * layer + 2))
            gather()
            with pe.Fori(0, PAIRS) as i:
                pe.wait_ge(m["xT_ready"], n17 + i + 1)
                for bank, w in ((GATE, 0), (UP, 2)):
                    wa = unit(i, w).rearrange("p (c n) -> p c n", c=KC)
                    wb = unit(i, w + 1).rearrange("p (c n) -> p c n", c=KC)
                    for c in range(KC):
                        pe.matmul(psum[0:SLOTS, bank, :], xT[:, c, 0:SLOTS], wa[:, c, :],
                                       start=c == 0, stop=c == KC - 1)
                        mm = pe.matmul(psum[SLOTS:P, bank, :], xT[:, c, SLOTS:P], wb[:, c, :],
                                       start=c == 0, stop=c == KC - 1)
                    mm.then_inc(used, 2)
                pe.wait_ge(m["y_ready"], 2 * (n17 + i + 1))
                spread_back()
                pe.wait_ge(m["sel_ready"], n17 + i + 2)
                gather()
                pe.wait_ge(m["act_ready"], n16 + i + 1)
                for c in range(FC):
                    pe.transpose(psum[:, GATE, c * P:(c + 1) * P], act_h[:, c, :], ident)
                for tc in range(TC):
                    mm = pe.transpose(psum[:, UP, tc * P:(tc + 1) * P], selw[:, tc, :], ident)
                mm.then_inc(m["turned"], 1)
                pe.wait_ge(m["actT_ready"], n16 + i + 1)
                pe.wait_ge(m["xT_ready"], n17 + i + 2)
                wa = unit(i, 4).rearrange("p (c n) -> p c n", c=FC)
                wb = unit(i, 5).rearrange("p (c n) -> p c n", c=FC)
                for n in range(2):
                    for c in range(FC):
                        pe.matmul(psum[0:SLOTS, YB + n, :], actT[:, c, 0:SLOTS],
                                       wa[:, c, 512 * n:512 * (n + 1)], start=c == 0, stop=c == FC - 1)
                        mm = pe.matmul(psum[SLOTS:P, YB + n, :], actT[:, c, SLOTS:P],
                                       wb[:, c, 512 * n:512 * (n + 1)], start=c == 0, stop=c == FC - 1)
                mm.then_inc(used, 2)
            pe.wait_ge(m["y_ready"], 2 * (n17 + PAIRS + 1))
            spread_back()

        def moe_act(act, layer, over, rnd):
            m = M[layer]
            n17, n16 = rnd * (PAIRS + 1), rnd * PAIRS

            def keep_gathered():
                nc.scalar.copy(xT, psum[:, YB:YB + 2, :].rearrange("p b (c s) -> p (b c) s", s=P)).then_inc(m["xT_ready"], 1)

            act.wait_ge(m["gathered"], n17 + 1)
            keep_gathered()
            with act.Fori(0, PAIRS) as i:
                wait_pair(act, layer, rnd, i, 2)
                nc.scalar.activation(sig, psum[:, GATE, :], ACT.Sigmoid).then_inc(m["sig_ready"], 1)
                act.wait_ge(m["gathered"], n17 + i + 2)
                keep_gathered()
                act.wait_ge(m["turned"], n16 + i + 1)
                nc.scalar.copy(actT, psum[:, GATE, :].rearrange("p (c s) -> p c s", c=FC))
                nc.scalar.copy(spread, psum[:, UP, 0:TC * P].rearrange("p (c s) -> p c s", c=TC)).then_inc(m["actT_ready"], 1)
                wait_pair(act, layer, rnd, i, 6)
                nc.scalar.copy(y_sb[:, 0:512], psum[:, YB, :]).then_inc(m["y_ready"], 1)

        def clear_outputs(layer):
            nc.vector.memset(y_sb, 0.0).then_inc(M[layer]["y_ready"], 1)
            nc.vector.memset(flat(spread), 0.0).then_inc(M[layer]["y_ready"], 1)

        def moe_dve(dve, layer, over, rnd, after_one_hots=None):
            m = M[layer]
            n17, n16 = rnd * (PAIRS + 1), rnd * PAIRS
            STEPS = 1

            def one_hots(pair):
                for e in range(2):
                    for tc in range(TC):
                        r = nc.vector.tensor_scalar(sel[:, tc, e * SLOTS:(e + 1) * SLOTS], const("iota"),
                                                    rank[:, tc, bass.ds(pair * 2 + e, 1)], small[:, 2 + tc:3 + tc],
                                                    ALU.is_equal, ALU.mult)
                r.then_inc(m["sel_ready"], 1)

            def weighted(pair):
                for e in range(2):
                    for tc in range(TC):
                        r = nc.vector.tensor_scalar(selw[:, tc, e * SLOTS:(e + 1) * SLOTS], const("iota"),
                                                    rank[:, tc, bass.ds(pair * 2 + e, 1)],
                                                    wtab[:, tc, bass.ds(pair * 2 + e, 1)], ALU.is_equal, ALU.mult)
                return r

            if after_one_hots is None:
                clear_outputs(layer)
            one_hots(0)
            if after_one_hots is not None:
                after_one_hots(layer)
            weighted(0)
            with dve.Fori(0, PAIRS) as i:
                turn = InTurn(dve, m["turn"], (n16 + i) * STEPS)
                dve.wait_ge(m["gathered"], n17 + i + 1)
                one_hots(i + 1)
                dve.wait_ge(m["sig_ready"], n16 + i + 1)
                turn(nc.vector.tensor_tensor(sig, psum[:, GATE, :], sig, ALU.mult))
                assert turn.n == STEPS
                wait_pair(dve, layer, rnd, i, 4)
                nc.vector.tensor_tensor(act_h.rearrange("p c s -> p s c"), psum[:, UP, :].rearrange("p (s c) -> p s c", c=FC),
                                        sig.rearrange("p (s c) -> p s c", c=FC), ALU.mult).then_inc(m["act_ready"], 1)
                dve.wait_ge(m["turned"], n16 + i + 1)
                weighted(i + 1)
                wait_pair(dve, layer, rnd, i, 6)
                nc.vector.tensor_copy(y_sb[:, 512:1024], psum[:, YB + 1, :]).then_inc(m["y_ready"], 1)
            dve.wait_ge(m["spread_done"], n17 + PAIRS + 1)
            for tc in range(TC):
                r = nc.vector.tensor_tensor(x[:, tc, :], x[:, tc, :], flat(psum[:, 2 * tc:2 * tc + 2, :]), ALU.add)
            and_wait(dve, r, m["added"], rnd + 1)

        roots_asked, roots_taken = [], []

        def inverse_root(dve, instruction, turn, col, count):
            assert ROOTS[len(roots_asked)] == (col, count)
            roots_asked.append((col, count))
            instruction.then_inc(S["root_in"], 1)
            dve.wait_ge(S["root_out"], len(roots_asked))
            v, y, z = small[:, col:col + count], small[:, 64:64 + count], small[:, 80:80 + count]
            turn(nc.vector.tensor_tensor(z, y, y, ALU.mult))
            turn(nc.vector.tensor_tensor(z, z, v, ALU.mult))
            turn(nc.vector.tensor_scalar(z, z, -0.5, 1.5, ALU.mult, ALU.add))
            turn(nc.vector.tensor_tensor(v, y, z, ALU.mult))

        def take_root(act, turn):
            col, count = ROOTS[len(roots_taken)]
            roots_taken.append(col)
            act.wait_ge(S["root_in"], len(roots_taken))
            y = small[:, 64:64 + count]
            turn(nc.scalar.activation(y, small[:, col:col + count], ACT.Ln))
            nc.scalar.activation(y, y, ACT.Exp, scale=-0.5).then_inc(S["root_out"], 1)

        def norm_act(act, n):
            for tc in range(TC):
                if n % 2 == 1:
                    act.wait_ge(S["added"], (n - 1) + tc + 1)
                nc.scalar.activation(mixed[:, tc, :], x[:, tc, :], ACT.Square,
                                     accum_out=small[:, tc:tc + 1]).then_inc(S["squares"], 1)

        def norm_root(dve, turn, n):
            dve.wait_ge(S["squares"], TC * (n + 1))
            inverse_root(dve, nc.vector.tensor_scalar(small[:, 2:4], small[:, 0:2], 1.0 / D, EPS, ALU.mult, ALU.add), turn, 2, 2)

        def norm_apply(dve, n):
            dve.wait_ge(S["gain_landed"], 16 * (n + 1))
            for tc in range(TC):
                nc.vector.scalar_tensor_tensor(
                    h[:, tc].rearrange("p c q -> p q c"), x[:, tc, :].rearrange("p (q c) -> p q c", c=KC),
                    small[:, 2 + tc:3 + tc], gain[:, :].rearrange("p (q c) -> p q c", c=KC),
                    ALU.mult, ALU.mult).then_inc(S["normed"], 1)
            dve.wait_ge(S["normed"], TC * (n + 1))
            nc.vector.memset(small[:, 4:5], 0.0).then_inc(S["gain_used"], 1)

        def turn_h(pe, n):
            for tc in range(TC):
                pe.wait_ge(S["added"] if n % 2 else S["normed"], TC * (n // 2 if n % 2 else n) + tc + 1)
                for c in range(KC):
                    src = x[:, tc, c * P:(c + 1) * P] if n % 2 else h[:, tc, c, :]
                    mm = pe.transpose(psum[:, c // 2, (c % 2) * SEQ + tc * P:(c % 2) * SEQ + (tc + 1) * P], src, ident)
            mm.then_inc(S["h_turned"], 1)

        def turn_mixed(pe, half):
            for tc in range(TC):
                for c in range(4):
                    mm = pe.transpose(psum[:, c // 2, (c % 2) * SEQ + tc * P:(c % 2) * SEQ + (tc + 1) * P],
                                      mixed[:, tc, (4 * half + c) * P:(4 * half + c + 1) * P], ident)
            mm.then_inc(S["mix_turned"], 1)

        def keep_mixT(half, copy):
            return copy(hT[:, 4 * half:4 * half + 4, :].rearrange("p (b c) t -> p b (c t)", b=2), psum[:, 0:2, :])

        def keep_hT(half, copy):
            return copy(hT[:, 4 * half:4 * half + 4, :].rearrange("p (b c) t -> p b (c t)", b=2),
                        psum[:, 2 * half:2 * half + 2, :])

        @block.tensor
        def _(pe):
            def project(layer, n):
                g = (0, UNITS_IN[0])[layer] + n
                u = unit_base(layer) + n
                wait_unit(pe, u)
                if g >= 2:
                    pe.wait_ge(proj_used[g % 2], g // 2)
                w = ring[:, u % RING, :].rearrange("p (c n) -> p c n", c=KC)
                banks = proj(g)
                if BLOCKS[layer][n] in TURNED[layer]:
                    for m in range(HEADS):
                        for c in range(KC):
                            mm = pe.matmul(banks[:, m // 2, (m % 2) * SEQ:(m % 2 + 1) * SEQ],
                                           w[:, c, m * P:(m + 1) * P], hT[:, c, :], start=c == 0, stop=c == KC - 1)
                else:
                    for tc in range(TC):
                        for c in range(KC):
                            mm = pe.matmul(banks[:, tc, :], hT[:, c, tc * P:(tc + 1) * P], w[:, c, :],
                                           start=c == 0, stop=c == KC - 1)
                mm.then_inc(S["unit_used"], 1)

            def causal(bank, q, k):
                pe.matmul(psum[:, bank, 0:SEQ], k[:, 0:P], q, start=True, stop=True)
                return pe.matmul(psum[:, bank, SEQ:TRI], k[:, P:SEQ], q[:, P:SEQ], start=True, stop=True)

            def attend(bank, hd, s, v):
                cols = slice(hd * HD, (hd + 1) * HD)
                pe.matmul(psum[:, bank, cols], s[:, 0:P], v[:, 0, cols], start=True, stop=True)
                pe.matmul(psum[:, bank + 1, cols], s[:, P:SEQ], v[:, 0, cols], start=True, stop=False)
                mm = pe.matmul(psum[:, bank + 1, cols], s[:, SEQ:TRI], v[:, 1, cols], start=False, stop=True)
                mm.then_inc(S["pv_done"], 1)

            def turn_roped(col):
                for hd in range(HEADS):
                    for tc in range(TC):
                        mm = pe.transpose(psum[:, 6 + hd // 2, (hd % 2) * SEQ + tc * P:(hd % 2) * SEQ + (tc + 1) * P],
                                          mixed[:, tc, col + hd * HD:col + (hd + 1) * HD], ident)
                mm.then_inc(S["turned"], 1)

            def project_out(layer):
                for half in range(2):
                    pe.wait_ge(S["gated"], 2 * layer + half + 1)
                    if half == 0:
                        pe.wait_ge(proj_used[0], (4, 7)[layer])
                    turn_mixed(pe, half)
                    pe.wait_ge(S["mixT_ready"], 2 * layer + half + 1)
                    u = unit_base(layer) + UNITS_IN[layer] + half
                    wait_unit(pe, u)
                    w = ring[:, u % RING, :].rearrange("p (c n) -> p c n", c=4)
                    for tc in range(TC):
                        for c in range(4):
                            for n in range(2):
                                mm = pe.matmul(psum[:, 4 + 2 * tc + n, :], hT[:, 4 * half + c, tc * P:(tc + 1) * P],
                                               w[:, c, 512 * n:512 * (n + 1)], start=half == 0 and c == 0,
                                               stop=half == 1 and c == 3)
                        if half == 1 and tc == 0:
                            mm.then_inc(S["out_first"], 1)
                    mm.then_inc(S["unit_used"], 1)

            def route_and_experts(layer):
                n = 2 * layer + 1
                turn_h(pe, n)
                pe.wait_ge(S["hT_ready"], 2 * (n + 1))
                pe.wait_ge(S["router_ready"], 2)
                for tc in range(TC):
                    for c in range(KC):
                        mm = pe.matmul(psum[:, 4, tc * 36:(tc + 1) * 36], hT[:, c, tc * P:(tc + 1) * P],
                                       rw[:, layer, c, :], start=c == 0, stop=c == KC - 1)
                mm.then_inc(S["logits_done"], 1)
                pe.wait_ge(S["picked_ready"], layer + 1)
                pe.matmul(psum[:, 5, 0:32], before, picked[:, 0, :], start=True, stop=True)
                pe.matmul(psum[:, 5, 32:64], before, picked[:, 1, :], start=True, stop=False)
                pe.matmul(psum[:, 5, 32:64], ones[:, 0:P], picked[:, 0, :], start=False, stop=True)
                pe.matmul(psum[:, 5, 64:96], ones[:, 0:P], picked[:, 0, :], start=True, stop=False)
                mm = pe.matmul(psum[:, 5, 64:96], ones[:, 0:P], picked[:, 1, :], start=False, stop=True)
                mm.then_inc(S["ranks_done"], 1)
                moe_pe(pe, layer, 0, 0)
                with pe.If(pe.value_load(over_i[0:1, layer:layer + 1], min_val=0, max_val=SEQ) > SLOTS):
                    with pe.Fori(0, OVER_ROUNDS) as r:
                        moe_pe(pe, layer, 1, r + 1)
                with pe.Else():
                    pe.nop()

            pe.wait_ge(S["first_landed"], 16)
            turn_h(pe, 0)
            pe.wait_ge(S["hT_ready"], 2)
            k = 0

            def next_scores():
                nonlocal k
                if k >= 2:
                    pe.wait_ge(S["st_ready"], k - 1)
                k += 1
                return 4 + (k - 1) % 2

            def scores_hgrn(hd):
                pe.wait_ge(S["qe_ready"], 1)
                pe.wait_ge(S["ke_ready"], hd + 1)
                bank = next_scores()
                for i in range(NSUB):
                    q = q2T[:, hd, i * SUB:(i + 1) * SUB]
                    mm = pe.matmul(psum[:, bank, i * SUB:(i + 1) * SUB], ke0[:, i, :], q, start=True, stop=True)
                    if i >= NSUB // 2:
                        mm = pe.matmul(psum[:, bank, SEQ - P + i * SUB:SEQ - P + (i + 1) * SUB], ke1[:, i - NSUB // 2, :], q,
                                       start=True, stop=True)
                mm.then_inc(S["scores_done"], 1)

            def scores_ret(hd):
                bank = next_scores()
                causal(bank, qT[:, hd, :], kT[:, hd, :]).then_inc(S["scores_done"], 1)

            for n in range(4):
                project(0, n)
            scores_hgrn(0)
            pe.wait_ge(S["roped"], 1)
            turn_roped(0)
            project(0, 4)
            scores_hgrn(1)
            pe.wait_ge(S["turned_sb"], 1)
            pe.wait_ge(S["roped"], 2)
            turn_roped(GROUP_W)
            project(0, 5)
            scores_hgrn(2)
            pe.wait_ge(S["turned_sb"], 2)
            pe.wait_ge(S["val_ready"], 1)
            scores_ret(0)
            scores_ret(1)
            for hd in range(HEADS):
                pe.wait_ge(S["st_ready"], 3 + hd + 1)
                attend(6, hd, st[:, hd % 2, :], val)
                if hd + 2 < HEADS:
                    scores_ret(hd + 2)
            scores_hgrn(3)
            project(0, 6)
            pe.wait_ge(S["val_ready"], 2)
            pe.wait_ge(S["st_ready"], 2 * HEADS)
            for hd in range(HEADS):
                attend(4, hd, st2[:, hd, :], val2)
            project(0, 7)
            pe.wait_ge(S["out_used"], 2)
            project_out(0)
            route_and_experts(0)

            turn_h(pe, 2)
            pe.wait_ge(S["hT_ready"], 6)

            def stick_scores(hd):
                if hd >= 1:
                    pe.wait_ge(S["stick_abs"], hd)
                else:
                    pe.wait_ge(S["turned_sb"], 4)
                causal(4, qT[:, hd, :], kT[:, hd, :]).then_inc(S["scores_done"], 1)

            def stick_sums(hd):
                pe.wait_ge(S["stick_l"], hd + 1)
                if hd >= 1:
                    pe.wait_ge(S["stick_arg"], hd)
                pe.matmul(psum[:, 5, 0:SEQ], from_on, sbl[:, 0:SEQ], start=True, stop=False, skip_group_check=True)
                pe.matmul(psum[:, 5, P:SEQ], ones[:, 0:P], sbl[:, SEQ:TRI], start=False, stop=True, skip_group_check=True)
                mm = pe.matmul(psum[:, 5, SEQ:TRI], from_on, sbl[:, SEQ:TRI], start=True, stop=True, skip_group_check=True)
                mm.then_inc(S["stick_r"], 1)

            def diff_scores(hd):
                if hd >= 1:
                    pe.wait_ge(S["diff_in"], hd)
                for part_ in range(2):
                    rows = slice(64 * part_, 64 * part_ + 64)
                    pe.matmul(psum[:, 6 + part_, 0:P], q2T[rows, hd, 0:P], k2T[rows, hd, 0:P], start=True, stop=True)
                    mm = pe.matmul(psum[:, 6 + part_, P:TRI], q2T[rows, hd, P:SEQ], k2T[rows, hd, :], start=True, stop=True)
                mm.then_inc(S["scores_done"], 1)

            def diff_turn(hd):
                pe.wait_ge(S["diff_a"], hd + 1)
                if hd >= 2:
                    pe.wait_ge(S["diff_aT"], hd - 1)
                a = dff[:, hd % 2, :]
                pe.transpose(psum[:, hd % 2, 0:P], a[:, 0:P], ident)
                pe.transpose(psum[:, hd % 2, P:SEQ], a[:, P:SEQ], ident)
                pe.transpose(psum[:, hd % 2, SEQ:TRI], a[:, SEQ:TRI], ident).then_inc(S["diff_turned"], 1)

            project(1, 0)
            project(1, 1)
            stick_scores(0)
            project(1, 2)
            stick_sums(0)
            stick_scores(1)
            project(1, 3)
            stick_sums(1)
            stick_scores(2)
            pe.wait_ge(S["roped"], 3)
            turn_roped(0)
            project(1, 4)
            stick_sums(2)
            stick_scores(3)
            pe.wait_ge(S["turned_sb"], 5)
            pe.wait_ge(S["roped"], 4)
            turn_roped(GROUP_W)
            pe.wait_ge(S["turned_sb"], 6)
            diff_scores(0)
            project(1, 5)
            stick_sums(3)
            diff_scores(1)
            pe.wait_ge(S["val_ready"], 4)
            pe.wait_ge(S["stick_a"], HEADS)
            for hd in range(HEADS):
                attend(4, hd, sta[:, hd, :], val)
            for g in range(2):
                pe.wait_ge(proj_used[g], 7)
            for hd in range(HEADS):
                diff_turn(hd)
                if hd + 2 < HEADS:
                    diff_scores(hd + 2)
                pe.wait_ge(S["diff_aT"], hd + 1)
                attend(2, hd, st[:, hd % 2, :], val2)
            project_out(1)
            route_and_experts(1)

        @block.scalar
        def _(act):
            turn = InTurn(act, S["act_turn"])

            def take_over_rounds(layer):
                with act.If(act.value_load(over_i[0:1, layer:layer + 1], min_val=0, max_val=SEQ) > SLOTS):
                    with act.Fori(0, OVER_ROUNDS) as r:
                        moe_act(act, layer, 1, r + 1)
                with act.Else():
                    act.nop()

            def keep_turned(dst, n):
                act.wait_ge(S["turned"], n)
                nc.scalar.copy(dst.rearrange("p (b a) t -> p b (a t)", b=2), psum[:, 6:8, :]).then_inc(S["turned_sb"], 1)

            def hT_half(n):
                act.wait_ge(S["h_turned"], n + 1)
                keep_hT(0, nc.scalar.copy).then_inc(S["hT_ready"], 1)

            def finish_mixer(layer):
                act.wait_ge(S["mix_turned"], 2 * layer + 1)
                keep_mixT(0, nc.scalar.copy).then_inc(S["mixT_ready"], 1)
                nc.scalar.preload_act_table_set(LOG_EXP)
                norm_act(act, 2 * layer + 1)
                hT_half(2 * layer + 1)
                take_root(act, turn)

            def route(layer):
                act.wait_ge(S["group_max"], layer + 1)
                nc.scalar.activation(rt[:, 0:8], rt[:, 0:8], ACT.Exp).then_inc(S["group_exp"], 1)
                act.wait_ge(S["top_diff"], layer + 1)
                nc.scalar.activation(rt[:, 8:10], rt[:, 8:10], ACT.Exp).then_inc(S["top_exp"], 1)
                nc.scalar.preload_act_table(ACT.Sigmoid)

            def keep_values(dst, g, ready):
                wait_projected(act, g + 1)
                nc.scalar.copy(flat(dst), flat(proj(g))).then_inc(S["val_ready"], 1)
                act.wait_ge(S["val_ready"], ready)
                nc.scalar.copy(small[0:1, 61:62], small[0:1, 60:61]).then_inc(proj_used[g % 2], 1)

            nc.scalar.preload_act_table_set(LOG_EXP)
            act.wait_ge(S["x_landed"], 16)
            norm_act(act, 0)
            take_root(act, turn)
            hT_half(0)
            act.wait_ge(S["rope_args"], 1)
            turn(nc.scalar.activation(cos_t, sin_t, ACT.Sin, scale=0.5))
            nc.scalar.activation(sin_t, sin_t, ACT.Sin).then_inc(S["rope_ready"], 1)
            act.wait_ge(S["lb_in"], 1)
            nc.scalar.activation(lbt[:, :, :], lbt[:, :, :], ACT.Exp).then_inc(S["lb_exp"], 1)
            wait_projected(act, 1)
            nc.scalar.activation(tmp, flat(proj(0)), ACT.Sigmoid)
            nc.scalar.activation(flat(cumf), flat(proj(0)), ACT.Sigmoid, scale=-1.0).then_inc(S["f_sig"], 1)
            act.wait_ge(S["f_sig"], 1)
            turn(nc.scalar.copy(small[0:1, 60:61], small[0:1, 0:1]))
            nc.scalar.copy(small[0:1, 61:62], small[0:1, 60:61]).then_inc(proj_used[0], 1)
            nc.scalar.preload_act_table_set(LOG_EXP)
            act.wait_ge(S["f_ready"], 1)
            nc.scalar.activation(tmp, tmp, ACT.Ln).then_inc(S["f_log"], 1)
            nc.scalar.activation(flat(k2T), flat(k2T), ACT.Ln).then_inc(S["f_log"], 1)
            wait_projected(act, 2)
            nc.scalar.activation(flat(q2T), flat(proj(1)), ACT.Sigmoid).then_inc(S["q_sig"], 1)
            nc.scalar.preload_act_table_set(LOG_EXP)
            act.wait_ge(S["mid_in"], 1)
            nc.scalar.activation(tmp, tmp, ACT.Exp).then_inc(S["mid_exp"], 1)

            def decayed_keys(hd):
                if hd == 0:
                    act.wait_ge(S["zeroed"], 1)
                    act.wait_ge(S["keys_log"], 1)
                else:
                    act.wait_ge(S["scores_done"], hd)
                for dst, s0, i0 in ((ke0, 0, 0), (ke1, P, NSUB // 2)):
                    for i in range(i0, NSUB):
                        n = min(P, SUB * (i + 1) - s0)
                        ins = nc.scalar.activation(dst[:, i - i0, 0:n], k2T[:, hd, s0:s0 + n], ACT.Exp, scale=-1.0,
                                                   bias=cumf[:, hd, SUB * i + SUB // 2 - 1:SUB * i + SUB // 2])
                ins.then_inc(S["ke_ready"], 1)

            decayed_keys(0)
            decayed_keys(1)
            keep_turned(qT, 1)
            keep_values(val, 4, 1)
            decayed_keys(2)
            keep_turned(kT, 2)
            keep_values(val2, 5, 2)
            decayed_keys(3)
            act.wait_ge(S["pv_done"], HEADS)
            nc.scalar.activation(tmp, flat(psum[:, 6:8, :]), ACT.Square).then_inc(S["sq_out"], 1)
            take_root(act, turn)
            wait_projected(act, 7)
            nc.scalar.activation(flat(kT), flat(proj(6)), ACT.Sigmoid).then_inc(S["gate_sig"], 1)
            nc.scalar.preload_act_table_set(LOG_EXP)
            act.wait_ge(S["pv_done"], 2 * HEADS)
            nc.scalar.activation(tmp, flat(psum[:, 4:6, :]), ACT.Square).then_inc(S["sq_out"], 1)
            take_root(act, turn)
            wait_projected(act, 8)
            nc.scalar.activation(flat(qT), flat(proj(7)), ACT.Sigmoid).then_inc(S["gate_sig"], 1)
            finish_mixer(0)
            route(0)
            moe_act(act, 0, 0, 0)
            take_over_rounds(0)

            nc.scalar.preload_act_table_set(LOG_EXP)
            act.wait_ge(S["finished_first"], 1)
            norm_act(act, 2)
            take_root(act, turn)
            hT_half(2)
            act.wait_ge(S["lam_dot"], 1)
            nc.scalar.activation(small[:, 40:42], small[:, 40:42], ACT.Exp).then_inc(S["lam_exp"], 1)
            for n in range(2):
                wait_projected(act, 9 + n)
                nc.scalar.copy((qT, kT)[n].rearrange("p h t -> p (h t)"), flat(proj(8 + n))).then_inc(S["turned_sb"], 1)
                act.wait_ge(S["turned_sb"], 3 + n)
                nc.scalar.copy(small[0:1, 61:62], small[0:1, 60:61]).then_inc(proj_used[n], 1)

            def stick_softplus(hd):
                act.wait_ge(S["stick_abs"], hd + 1)
                turn(nc.scalar.activation(sbe, sbe, ACT.Exp, scale=-1.0))
                nc.scalar.activation(sbe, sbe, ACT.Ln, bias=1.0).then_inc(S["stick_log"], 1)

            def stick_exp(hd):
                act.wait_ge(S["stick_arg"], hd + 1)
                nc.scalar.activation(sta[:, hd, :], sta[:, hd, :], ACT.Exp).then_inc(S["stick_a"], 1)

            def diff_squares(n):
                wait_projected(act, 11 + n)
                if n == 1:
                    act.wait_ge(S["roped"], 3)
                nc.scalar.activation(tmp1, flat(proj(10 + n)), ACT.Square).then_inc(S["norm_sq"], 1)

            def diff_exp(hd):
                act.wait_ge(S["diff_max"], hd + 1)
                s = dss[:, hd % 2]
                at = 16 * (hd % 2)
                for tc, cols in enumerate((slice(0, P), slice(P, TRI))):
                    for c in range(2):
                        j = at + 2 * tc + c
                        ins = nc.scalar.activation(s[:, c, cols], s[:, c, cols], ACT.Exp, bias=small[:, 8 + j:9 + j],
                                                   accum_out=small[:, 12 + j:13 + j])
                ins.then_inc(S["diff_exp"], 1)

            def diff_keep(hd):
                act.wait_ge(S["diff_turned"], hd + 1)
                nc.scalar.copy(st[:, hd % 2, :], psum[:, hd % 2, 0:TRI]).then_inc(S["diff_aT"], 1)

            stick_softplus(0)
            stick_exp(0)
            diff_squares(0)
            stick_softplus(1)
            take_root(act, turn)
            stick_exp(1)
            diff_squares(1)
            stick_softplus(2)
            take_root(act, turn)
            keep_turned(q2T, 3)
            stick_exp(2)
            keep_values(val2, 12, 3)
            stick_softplus(3)
            keep_turned(k2T, 4)
            diff_exp(0)
            keep_values(val, 13, 4)
            stick_exp(3)
            diff_exp(1)
            for hd in range(HEADS):
                if hd >= 2:
                    act.wait_ge(S["pv_done"], 3 * HEADS + hd - 1)
                diff_keep(hd)
                if hd + 2 < HEADS:
                    diff_exp(hd + 2)
            act.wait_ge(S["pv_done"], 4 * HEADS)
            nc.scalar.activation(tmp1, flat(psum[:, 2:4, :]), ACT.Square).then_inc(S["sq_out"], 1)
            take_root(act, turn)
            finish_mixer(1)
            route(1)
            moe_act(act, 1, 0, 0)
            take_over_rounds(1)

        @block.gpsimd
        def _(pool):
            pool.wait_ge(S["h_turned"], 1)
            nc.gpsimd.memset(ke0, 0.0)
            nc.gpsimd.memset(ke1, 0.0).then_inc(S["zeroed"], 1)
            for layer in range(2):
                pool.wait_ge(S["gain_landed"], 16 * (2 * layer + 2))
                for tc in range(TC):
                    pool.wait_ge(S["added"], 2 * layer + tc + 1)
                    nc.gpsimd.tensor_tensor(
                        h[:, tc].rearrange("p c q -> p q c"), x[:, tc, :].rearrange("p (q c) -> p q c", c=KC),
                        gain[:, :].rearrange("p (q c) -> p q c", c=KC), ALU.mult).then_inc(S["normed"], 1)
                pool.wait_ge(S["normed"], TC * (2 * layer + 2))
                nc.gpsimd.memset(small[:, 62 + layer:63 + layer], 0.0).then_inc(S["gain_used"], 1)

        @block.vector
        def _(dve):
            turn = InTurn(dve, S["dve_turn"])
            V = nc.vector

            def hT_half(n):
                dve.wait_ge(S["h_turned"], n + 1)
                keep_hT(1, V.tensor_copy).then_inc(S["hT_ready"], 1)

            def finish_mixer(layer):
                dve.wait_ge(S["mix_turned"], 2 * layer + 2)
                keep_mixT(1, V.tensor_copy).then_inc(S["mixT_ready"], 1)
                for tc in range(TC):
                    if tc == 0:
                        dve.wait_ge(S["out_first"], layer + 1)
                    else:
                        dve.wait_ge(S["unit_used"], moe_base(layer))
                    V.tensor_tensor(x[:, tc, :], x[:, tc, :], flat(psum[:, 4 + 2 * tc:6 + 2 * tc, :]),
                                    ALU.add).then_inc(S["added"], 1)
                dve.wait_ge(S["added"], 2 * layer + 2)
                hT_half(2 * layer + 1)
                norm_root(dve, turn, 2 * layer + 1)

            def rope_by_head(src, dst, width, cols, t1, t2):
                half = width // 2
                n = GROUP_W // width
                x1, x2 = src[:, :, :, 0:half], src[:, :, :, half:width]
                for_all = lambda tab: tab[:, :, cols].unsqueeze(2).broadcast_to([P, TC, n, half])
                c, s = for_all(cos_t), for_all(sin_t)
                turn(V.tensor_tensor(t1, x1, c, ALU.mult))
                turn(V.tensor_tensor(t2, x2, s, ALU.mult))
                turn(V.tensor_tensor(dst[:, :, :, 0:half], t1, t2, ALU.subtract))
                turn(V.tensor_tensor(t1, x2, c, ALU.mult))
                turn(V.tensor_tensor(t2, x1, s, ALU.mult))
                return V.tensor_tensor(dst[:, :, :, half:width], t1, t2, ALU.add)

            def inverse_rms(squares, col, count, width):
                r = small[:, col:col + count]
                turn(V.tensor_reduce(r, squares, AX, ALU.add))
                inverse_root(dve, V.tensor_scalar(r, r, 1.0 / width, EPS, ALU.mult, ALU.add), turn, col, count)
                return r

            def route(layer):
                def r3(at, n):
                    return rt[:, at:at + TC * n].rearrange("p (c n) -> p c n", c=TC)

                def over(a, n):
                    return a.unsqueeze(2).broadcast_to([P, TC, n])
                logits, gm, gs = r3(64, 36), rt[:, 10:12], rt[:, 12:14]
                g_hot, e_in, s32, hot1, hot2 = r3(160, 4), r3(192, 32), r3(256, 32), r3(320, 32), r3(384, 32)
                m1, m2, sc, pg = rt[:, 14:16], rt[:, 16:18], rt[:, 18:20], rt[:, 20:22]
                w1, w2 = rt[:, 22:24], rt[:, 24:26]
                gl = r3(0, 4)
                nc.vector.memset(wtab.rearrange("p c e -> p (c e)"), 0.0)
                nc.vector.memset(rank.rearrange("p c e -> p (c e)"), -1.0)
                clear_outputs(layer)
                dve.wait_ge(S["logits_done"], layer + 1)
                for tc in range(TC):
                    r = V.scalar_tensor_tensor(logits[:, tc], psum[:, 4, 36 * tc:36 * (tc + 1)], small[:, 2 + tc:3 + tc],
                                               rb[:, layer, :], ALU.mult, ALU.add)
                turn(r)
                turn(V.tensor_reduce(gm, logits[:, :, 0:4], AX, ALU.max))
                and_wait(dve, V.tensor_tensor(gl, logits[:, :, 0:4], over(gm, 4), ALU.subtract), S["group_max"], layer + 1)
                falling = const("falling").unsqueeze(1).broadcast_to([P, TC, 32])

                def one(a, tc):
                    return a[:, tc:tc + 1]

                def first_at(hot, values, top, n):
                    for tc in range(TC):
                        r = V.scalar_tensor_tensor(hot[:, tc], values[:, tc], one(top, tc), falling[:, tc, 0:n],
                                                   ALU.is_equal, ALU.mult)
                    turn(r)
                    turn(V.tensor_reduce(sc, hot, AX, ALU.max))
                first_at(g_hot, logits[:, :, 0:4], gm, 4)
                for tc in range(TC):
                    r = V.tensor_scalar(g_hot[:, tc], g_hot[:, tc], one(sc, tc), -1.0, ALU.is_equal, ALU.add)
                turn(r)
                by_group = e_in.rearrange("p c (g e) -> p c g e", g=N_GROUPS)
                for tc in range(TC):
                    r = V.scalar_tensor_tensor(by_group[:, tc], g_hot[:, tc, :].unsqueeze(2).broadcast_to([P, N_GROUPS, PER_GROUP]),
                                               BIG, logits[:, tc, 4:36].rearrange("p (g e) -> p g e", g=N_GROUPS),
                                               ALU.mult, ALU.add)
                turn(r)
                turn(V.tensor_reduce(m1, e_in, AX, ALU.max))
                first_at(hot1, e_in, m1, 32)
                for tc in range(TC):
                    V.tensor_scalar(s32[:, tc], hot1[:, tc], one(sc, tc), -BIG, ALU.is_equal, ALU.mult)
                    r = V.tensor_scalar(hot2[:, tc], hot1[:, tc], one(sc, tc), None, ALU.is_equal)
                turn(r)
                V.tensor_copy(hot1, hot2)
                turn(V.tensor_tensor(s32, s32, e_in, ALU.add))
                turn(V.tensor_reduce(m2, s32, AX, ALU.max))
                first_at(hot2, s32, m2, 32)
                for tc in range(TC):
                    r = V.scalar_tensor_tensor(picked[:, tc], hot2[:, tc], one(sc, tc), hot1[:, tc], ALU.is_equal, ALU.add)
                r.then_inc(S["picked_ready"], 1)
                V.tensor_tensor(rt[:, 8:10], m2, m1, ALU.subtract).then_inc(S["top_diff"], 1)
                dve.wait_ge(S["picked_ready"], layer + 1)
                turn(V.tensor_tensor(hot2, picked, hot1, ALU.subtract))
                dve.wait_ge(S["ranks_done"], layer + 1)
                turn(V.scalar_tensor_tensor(s32, psum[:, 5, 0:64].rearrange("p (c n) -> p c n", c=TC), 1.0, picked,
                                            ALU.add, ALU.mult))
                V.tensor_scalar(rank[:, :, 0:32], s32, -1.0, None, ALU.add)
                turn(V.tensor_reduce(sc[:, 0:1], psum[:, 5, 64:96], AX, ALU.max))
                and_wait(dve, V.tensor_copy(over_i[:, layer:layer + 1], sc[:, 0:1]), S["route_ready"], layer + 1)

            def gates(layer):
                def r3(at, n):
                    return rt[:, at:at + TC * n].rearrange("p (c n) -> p c n", c=TC)
                gl, gs, pg, w1, w2 = r3(0, 4), rt[:, 12:14], rt[:, 20:22], rt[:, 22:24], rt[:, 24:26]
                hot1, hot2 = r3(320, 32), r3(384, 32)
                dve.wait_ge(S["group_exp"], layer + 1)
                turn(V.tensor_reduce(gs, gl, AX, ALU.add))
                turn(V.reciprocal(pg, gs))
                dve.wait_ge(S["top_exp"], layer + 1)
                turn(V.tensor_scalar(w1, rt[:, 8:10], 1.0, None, ALU.add))
                turn(V.reciprocal(w1, w1))
                turn(V.tensor_tensor(w1, w1, pg, ALU.mult))
                turn(V.tensor_tensor(w2, w1, rt[:, 8:10], ALU.mult))
                for tc in range(TC):
                    r = V.tensor_scalar(hot1[:, tc], hot1[:, tc], w1[:, tc:tc + 1], None, ALU.mult)
                turn(r)
                for tc in range(TC):
                    r = V.scalar_tensor_tensor(wtab[:, tc, 0:32], hot2[:, tc], w2[:, tc:tc + 1], hot1[:, tc], ALU.mult, ALU.add)
                turn(r)

            def take_over_rounds(layer):
                with dve.If(dve.value_load(over_i[0:1, layer:layer + 1], min_val=0, max_val=SEQ) > SLOTS):
                    with dve.Fori(0, OVER_ROUNDS) as r:
                        m = M[layer]
                        V.tensor_scalar(rank[:, :, :], rank[:, :, :], -float(SLOTS), None, ALU.add).then_inc(m["round_done"], 1)
                        dve.wait_ge(m["round_done"], r + 1)
                        moe_dve(dve, layer, 1, r + 1)
                with dve.Else():
                    dve.nop()

            dve.wait_ge(S["x_landed"], 16)
            norm_root(dve, turn, 0)
            norm_apply(dve, 0)
            dve.wait_ge(S["first_landed"], 16)
            dve.wait_ge(S["pos_landed"], 16)
            hT_half(0)
            turn(V.tensor_copy(small[:, 5:7], pos_i[:, :]))
            for tc in range(TC):
                turn(V.tensor_scalar(sin_t[:, tc, :], const("inv_freq"), small[:, 5 + tc:6 + tc], None, ALU.mult))
            turn(V.tensor_scalar(cos_t, sin_t, 1 / (2 * math.pi), ROUND, ALU.mult, ALU.add))
            turn(V.tensor_scalar(cos_t, cos_t, -ROUND, None, ALU.add))
            turn(V.scalar_tensor_tensor(sin_t, cos_t, -TWO_PI_HI, sin_t, ALU.mult, ALU.add))
            turn(V.scalar_tensor_tensor(sin_t, cos_t, -TWO_PI_LO, sin_t, ALU.mult, ALU.add))
            and_wait(dve, V.tensor_scalar(sin_t, sin_t, 3.14159, -3.14159, ALU.min, ALU.max), S["rope_args"], 1)
            dve.wait_ge(S["lb_landed"], 16)
            lb4 = small[:, 44:48]
            turn(V.tensor_tensor(lb4, lbt[:, 0, :], lbt[:, 1, :], ALU.max))
            turn(V.tensor_tensor(lb4, lb4, lbt[:, 2, :], ALU.max))
            and_wait(dve, V.tensor_tensor(lbt[:, :, :], lbt[:, :, :], lb4.unsqueeze(1).broadcast_to([P, 3, HEADS]), ALU.subtract),
                     S["lb_in"], 1)
            dve.wait_ge(S["lb_exp"], 1)
            turn(V.tensor_tensor(lb4, lbt[:, 0, :], lbt[:, 1, :], ALU.add))
            turn(V.tensor_tensor(lb4, lb4, lbt[:, 2, :], ALU.add))
            turn(V.reciprocal(lb4, lb4))
            turn(V.tensor_tensor(lbw[:, 0, :], lbt[:, 0, :], lb4, ALU.mult))
            turn(V.tensor_scalar(lbw[:, 1, :], lbw[:, 0, :], -1.0, 1.0, ALU.mult, ALU.add))
            dve.wait_ge(S["rope_ready"], 1)
            turn(V.tensor_tensor(cos_t, cos_t, cos_t, ALU.mult))
            turn(V.tensor_scalar(cos_t, cos_t, -2.0, 1.0, ALU.mult, ALU.add))
            dve.wait_ge(S["f_sig"], 1)
            for hd in range(HEADS):
                cols = slice(hd * SEQ, (hd + 1) * SEQ)
                V.tensor_scalar(tmp[:, cols], tmp[:, cols], lbw[:, 1, hd:hd + 1], lbw[:, 0, hd:hd + 1], ALU.mult, ALU.add)
                r = V.tensor_scalar(k2T[:, hd, :], cumf[:, hd, :], lbw[:, 1, hd:hd + 1], K_FLOOR, ALU.mult, ALU.max)
            turn(r)
            and_wait(dve, V.tensor_scalar(tmp, tmp, F_FLOOR, None, ALU.max), S["f_ready"], 1)
            dve.wait_ge(S["f_log"], 1)
            dve.wait_ge(S["small_landed"], 16 * N_SMALL)
            for l in range(2):
                V.tensor_tensor(rw[:, l], rw[:, l], gcol[:, l, :].unsqueeze(2).broadcast_to([P, KC, 36]),
                                ALU.mult).then_inc(S["router_ready"], 1)
            for hd in range(HEADS):
                r = V.tensor_tensor_scan(cumf[:, hd, :], ones, tmp[:, hd * SEQ:(hd + 1) * SEQ], 0.0, ALU.mult, ALU.add)
            and_wait(dve, r, S["cum_ready"], 1)
            dve.wait_ge(S["f_log"], 2)
            and_wait(dve, V.tensor_tensor(flat(k2T), flat(cumf), flat(k2T), ALU.subtract), S["keys_log"], 1)
            sub = flat(cumf).rearrange("p (i s) -> p i s", s=SUB)
            and_wait(dve, V.tensor_tensor(tmp.rearrange("p (i s) -> p i s", s=SUB), sub,
                                          sub[:, :, SUB // 2 - 1].unsqueeze(2).broadcast_to([P, HEADS * NSUB, SUB]), ALU.subtract),
                     S["mid_in"], 1)
            dve.wait_ge(S["q_sig"], 1)
            and_wait(dve, V.tensor_tensor(flat(q2T), flat(proj(1)), flat(q2T), ALU.mult), proj_used[1], 1)
            dve.wait_ge(S["mid_exp"], 1)
            and_wait(dve, V.tensor_tensor(flat(q2T), flat(q2T), tmp, ALU.mult), S["qe_ready"], 1)

            def rope_ret(g, col):
                wait_projected(dve, g + 1)
                t12 = tmp.rearrange("p (a c h d) -> p a c h d", a=2, c=TC, h=HEADS)
                and_wait(dve, rope_by_head(heads(proj(g)), heads(mixed[:, :, col:col + GROUP_W]), HD, slice(0, 64),
                                           t12[:, 0], t12[:, 1]), S["roped"], g - 1)
                V.memset(small[:, 4:5], 0.0).then_inc(proj_used[g % 2], 1)

            def mask(k, dst, table):
                dve.wait_ge(S["scores_done"], k + 1)
                V.tensor_tensor(dst, psum[:, 4 + k % 2, 0:TRI], table, ALU.mult).then_inc(S["st_ready"], 1)

            def silu_gate(g, dst):
                dve.wait_ge(S["gate_sig"], g - 5)
                and_wait(dve, V.tensor_tensor(dst, flat(proj(g)), dst, ALU.mult), proj_used[g % 2], 4)

            def gated_norm(which, bank, col):
                dve.wait_ge(S["sq_out"], which + 1)
                r = inverse_rms(tmp.rearrange("p (n d) -> p n d", d=HD), 20 + 8 * which, 8, HD)
                out = mixed[:, :, col:col + GROUP_W]
                o = heads(psum[:, bank:bank + 2, :])
                and_wait(dve, V.tensor_tensor(heads(out), o, r.rearrange("p (c h) -> p c h", c=TC).unsqueeze(3)
                                              .broadcast_to([P, TC, HEADS, HD]), ALU.mult), S["out_used"], which + 1)
                g = retg[:, which, :].unsqueeze(1).broadcast_to([P, TC, GROUP_W])
                turn(V.tensor_tensor(out, out, g, ALU.mult))

            def gate_it(which, gate, col):
                out = mixed[:, :, col:col + GROUP_W]
                V.tensor_tensor(out, out, gate.rearrange("p h t -> p (h t)").rearrange("p (c n) -> p c n", c=TC),
                                ALU.mult).then_inc(S["gated"], 1)

            decay = lambda hd: const("decay")[:, hd * TRI:(hd + 1) * TRI]
            rope_ret(2, 0)
            mask(0, st2[:, 0, :], const("causal_scale"))
            rope_ret(3, GROUP_W)
            mask(1, st2[:, 1, :], const("causal_scale"))
            mask(2, st2[:, 2, :], const("causal_scale"))
            for hd in range(HEADS):
                if hd >= 2:
                    dve.wait_ge(S["pv_done"], hd - 1)
                mask(3 + hd, st[:, hd % 2, :], decay(hd))
            mask(7, st2[:, 3, :], const("causal_scale"))
            gated_norm(0, 6, 0)
            silu_gate(6, flat(kT))
            gate_it(0, kT, 0)
            gated_norm(1, 4, GROUP_W)
            silu_gate(7, flat(qT))
            gate_it(1, qT, GROUP_W)
            finish_mixer(0)
            route(0)
            moe_dve(dve, 0, 0, 0, gates)
            take_over_rounds(0)
            turn(V.memset(small[:, 4:5], 0.0))
            V.memset(small[:, 4:5], 0.0).then_inc(S["finished_first"], 1)

            norm_root(dve, turn, 2)
            norm_apply(dve, 2)
            hT_half(2)
            for i in range(2):
                turn(V.tensor_tensor(dlam[:, 2 * i, :], dlam[:, 2 * i, :], dlam[:, 2 * i + 1, :], ALU.mult))
                r = V.tensor_reduce(small[:, 40 + i:41 + i], dlam[:, 2 * i, :], AX, ALU.add)
            and_wait(dve, r, S["lam_dot"], 1)
            dve.wait_ge(S["lam_exp"], 1)
            neg_lam = small[:, 42:43]
            turn(V.tensor_tensor(neg_lam, small[:, 41:42], small[:, 40:41], ALU.subtract))
            turn(V.tensor_scalar(neg_lam, neg_lam, -LAM_INIT, None, ALU.add))

            def stick_in(hd):
                dve.wait_ge(S["scores_done"], 8 + hd + 1)
                turn(V.tensor_scalar(sbz[:, 0, :], psum[:, 4, 0:TRI], SCALE, None, ALU.mult))
                and_wait(dve, V.scalar_tensor_tensor(sbe, sbz[:, 0, :], -1.0, sbz[:, 0, :], ALU.mult, ALU.max), S["stick_abs"], hd + 1)

            def stick_l(hd):
                dve.wait_ge(S["stick_log"], hd + 1)
                turn(V.scalar_tensor_tensor(sbl, sbz[:, 0, :], 0.0, sbe, ALU.max, ALU.add))
                and_wait(dve, V.tensor_tensor(sbl, sbl, const("strict"), ALU.mult), S["stick_l"], hd + 1)
                turn(V.tensor_tensor(sbz[:, 1, :], sbz[:, 0, :], const("strict_add"), ALU.add))

            def stick_out(hd):
                dve.wait_ge(S["stick_r"], hd + 1)
                and_wait(dve, V.tensor_tensor(sta[:, hd, :], sbz[:, 1, :], psum[:, 5, 0:TRI], ALU.subtract),
                         S["stick_arg"], hd + 1)

            def qk_norm_rope(n):
                g = 10 + n
                dve.wait_ge(S["norm_sq"], n + 1)
                r = inverse_rms(tmp1.rearrange("p (n d) -> p n d", d=64), 44, 16, 64)
                by = lambda a: a.rearrange("p c (h d) -> p c h d", d=64)
                y = tmp1.rearrange("p (c n d) -> p c n d", c=TC, d=64)
                and_wait(dve, V.tensor_tensor(y, by(proj(g)), r.rearrange("p (c n) -> p c n", c=TC).unsqueeze(3)
                                              .broadcast_to([P, TC, 8, 64]), ALU.mult), proj_used[g % 2], 6)
                turn(V.tensor_tensor(tmp1.rearrange("p (n d) -> p n d", d=64), tmp1.rearrange("p (n d) -> p n d", d=64),
                                     dg[:, n, :].unsqueeze(1).broadcast_to([P, 16, 64]), ALU.mult))
                t12 = tmp2.rearrange("p (a c h d) -> p a c h d", a=2, c=TC, d=32)
                and_wait(dve, rope_by_head(y, by(mixed[:, :, n * GROUP_W:(n + 1) * GROUP_W]), 64, slice(64, 96),
                                           t12[:, 0], t12[:, 1]), S["roped"], 3 + n)

            def diff_in(hd):
                dve.wait_ge(S["scores_done"], (12, 13, 14, 15)[hd] + 1)
                s = dss[:, hd % 2]
                for c in range(2):
                    r = V.scalar_tensor_tensor(s[:, c, :], psum[:, 6 + c, 0:TRI], SCALE_DIFF, const("causal_add"),
                                               ALU.mult, ALU.add)
                and_wait(dve, r, S["diff_in"], hd + 1)
                at = 8 + 16 * (hd % 2)
                turn(V.tensor_reduce(small[:, at:at + 2], s[:, :, 0:P], AX, ALU.max))
                turn(V.tensor_reduce(small[:, at + 2:at + 4], s[:, :, P:TRI], AX, ALU.max))
                V.tensor_scalar(small[:, at:at + 4], small[:, at:at + 4], -1.0, None, ALU.mult).then_inc(S["diff_max"], 1)

            def diff_out(hd):
                dve.wait_ge(S["diff_exp"], hd + 1)
                if hd >= 2:
                    dve.wait_ge(S["diff_turned"], hd - 1)
                s, a = dss[:, hd % 2], dff[:, hd % 2, :]
                at = 12 + 16 * (hd % 2)
                turn(V.reciprocal(small[:, at:at + 4], small[:, at:at + 4]))
                for tc in range(TC):
                    k = small[:, at + 2 * tc + 1:at + 2 * tc + 2]
                    turn(V.tensor_tensor(k, k, neg_lam, ALU.mult))
                for tc, cols in enumerate((slice(0, P), slice(P, TRI))):
                    turn(V.tensor_scalar(a[:, cols], s[:, 0, cols], small[:, at + 2 * tc:at + 2 * tc + 1], None, ALU.mult))
                    r = V.scalar_tensor_tensor(a[:, cols], s[:, 1, cols], small[:, at + 2 * tc + 1:at + 2 * tc + 2],
                                               a[:, cols], ALU.mult, ALU.add)
                and_wait(dve, r, S["diff_a"], hd + 1)

            stick_in(0)
            for hd in range(HEADS):
                stick_l(hd)
                stick_out(hd)
                if hd + 1 < HEADS:
                    stick_in(hd + 1)
                if hd in (0, 1):
                    qk_norm_rope(hd)
                if hd == 2:
                    diff_in(0)
            diff_in(1)
            dve.wait_ge(S["pv_done"], 3 * HEADS)
            V.tensor_copy(mixed[:, :, 0:GROUP_W], psum[:, 4:6, :]).then_inc(S["gated"], 1)
            for hd in range(HEADS):
                diff_out(hd)
                if hd + 2 < HEADS:
                    diff_in(hd + 2)
            dve.wait_ge(S["sq_out"], 3)
            r = inverse_rms(tmp1.rearrange("p (n d) -> p n d", d=HD), 44, 8, HD)
            out = mixed[:, :, GROUP_W:D]
            turn(V.tensor_scalar(r, r, 1.0 - LAM_INIT, None, ALU.mult))
            turn(V.tensor_tensor(heads(out), heads(psum[:, 2:4, :]), r.rearrange("p (c h) -> p c h", c=TC).unsqueeze(3)
                                 .broadcast_to([P, TC, HEADS, HD]), ALU.mult))
            for tc in range(TC):
                r = V.tensor_tensor(mixed[:, tc, GROUP_W:D].rearrange("p (h d) -> p h d", d=HD),
                                    mixed[:, tc, GROUP_W:D].rearrange("p (h d) -> p h d", d=HD),
                                    subln[:, :].unsqueeze(1).broadcast_to([P, HEADS, HD]), ALU.mult)
            r.then_inc(S["gated"], 1)
            finish_mixer(1)
            route(1)
            moe_dve(dve, 1, 0, 0, gates)
            take_over_rounds(1)
            turn(V.memset(small[:, 4:5], 0.0))
            V.memset(small[:, 4:5], 0.0).then_inc(S["finished"], 1)


PARAMS = ["x", "positions", "norm_mix", "norm_ffn", "w_in_ab", "w_out_ab", "ret_gnorm", "hgrn_lb_logits",
          "hgrn_onorm", "w_in_cd", "w_out_cd", "diff_qnorm", "diff_knorm", "diff_lam_q1", "diff_lam_k1",
          "diff_lam_q2", "diff_lam_k2", "diff_subln", "router_group_w", "router_group_b",
          "router_expert_w", "router_expert_b", "w_gate", "w_up", "w_down"]


def kernel(**inputs):
    import concourse.bacc as bacc
    from concourse.bass_utils import run_bass_kernel_spmd

    nc = bacc.Bacc("TRN2", target_bir_lowering=False, num_devices=1)
    consts, where = shape_constants()
    arrays = {f"in_{n}": np.ascontiguousarray(inputs[n]) for n in PARAMS}
    arrays["in_consts"] = consts
    t = {n[3:]: nc.dram_tensor(n, a.shape, mybir.dt.from_np(a.dtype), kind="ExternalInput").ap()
         for n, a in arrays.items()}
    t["out"] = nc.dram_tensor("out", (1, SEQ, D), F32, kind="ExternalOutput").ap()
    build(nc, t, where, consts.shape[1])
    r = run_bass_kernel_spmd(nc, [arrays], core_ids=[0])
    return r.results[0]["out"]
```
